# Optimizing a Trainium2 kernel written in Bass

```python
import jax, jax.numpy as jnp
from jax import lax
import numpy as np

D_MODEL = 1024
BATCH = 1
SEQ = 256
DEPTH = 2

N_A = DEPTH // 2
N_B = DEPTH - N_A
HEAD_DIM = 64
MEM_LEN = 256
N_MEM_HEADS = 4
MEM_WIDTH = N_MEM_HEADS * HEAD_DIM
MIX_WIDTH = D_MODEL - MEM_WIDTH
CONV_CH = MIX_WIDTH
CONV_WIDTH = 31
N_FOX_HEADS = MIX_WIDTH // HEAD_DIM
D_FF = 2816
FFN_CONV_WIDTH = 3
BLOCK_Q = 128
RMS_EPS = 1e-6
LN_EPS = 1e-5


def rmsnorm(x, g):
    xf = x.astype(jnp.float32)
    y = xf * lax.rsqrt(jnp.mean(xf * xf, axis=-1, keepdims=True) + RMS_EPS)
    return (y * g.astype(jnp.float32)).astype(x.dtype)

def layernorm(x, g, b):
    xf = x.astype(jnp.float32)
    mu = jnp.mean(xf, axis=-1, keepdims=True)
    var = jnp.mean(jnp.square(xf - mu), axis=-1, keepdims=True)
    y = (xf - mu) * lax.rsqrt(var + LN_EPS)
    return (y * g.astype(jnp.float32) + b.astype(jnp.float32)).astype(x.dtype)

def causal_dwconv(x, w, b):
    width, ch = w.shape
    y = lax.conv_general_dilated(
        x, w[:, None, :].astype(x.dtype), window_strides=(1,),
        padding=((width - 1, 0),), dimension_numbers=("NWC", "WIO", "NWC"),
        feature_group_count=ch)
    return y + b

def conformer_conv(u, b_glu, w_dw, b_dw, ln_g, ln_b):
    u = u + b_glu
    a, gate = jnp.split(u, 2, axis=-1)
    v = a * jax.nn.sigmoid(gate)
    v = causal_dwconv(v, w_dw, b_dw)
    v = layernorm(v, ln_g, ln_b)
    return jax.nn.silu(v)

def memory_attention(q, mem_k, mem_v):
    b, s, _ = q.shape
    qh = q.reshape(b, s, N_MEM_HEADS, HEAD_DIM)
    kh = mem_k.reshape(b, -1, N_MEM_HEADS, HEAD_DIM)
    vh = mem_v.reshape(b, -1, N_MEM_HEADS, HEAD_DIM)
    logits = jnp.einsum("bshd,bmhd->bhsm", qh, kh).astype(jnp.float32) * (HEAD_DIM ** -0.5)
    p = jax.nn.softmax(logits, axis=-1).astype(vh.dtype)
    o = jnp.einsum("bhsm,bmhd->bshd", p, vh)
    return o.reshape(b, s, MEM_WIDTH)

def forgetting_attention(q, k, v, cum_logf):
    b, s, h, dh = q.shape
    scale = dh ** -0.5
    outs = []
    for i in range(s // BLOCK_Q):
        q0 = i * BLOCK_Q
        kend = q0 + BLOCK_Q
        qb = q[:, q0:kend]
        kb = k[:, :kend]
        vb = v[:, :kend]
        logits = jnp.einsum("bqhd,bkhd->bhqk", qb, kb).astype(jnp.float32) * scale
        logits = logits + cum_logf[:, :, q0:kend, None] - cum_logf[:, :, None, :kend]
        qpos = q0 + jnp.arange(BLOCK_Q)
        kpos = jnp.arange(kend)
        logits = jnp.where(kpos[None, :] <= qpos[:, None], logits, -jnp.inf)
        p = jax.nn.softmax(logits, axis=-1).astype(vb.dtype)
        outs.append(jnp.einsum("bhqk,bkhd->bqhd", p, vb))
    return jnp.concatenate(outs, axis=1)

def conv_ffn(h, w_up, w_dw, b_dw, w_down):
    u = h @ w_up
    u = causal_dwconv(u, w_dw, b_dw)
    gate, val = jnp.split(u, 2, axis=-1)
    return (jax.nn.silu(gate) * val) @ w_down

def first_inputs(seed: int = 0) -> dict:
    key = jax.random.key(seed)
    ks = jax.random.split(key, 24)
    f32 = jnp.float32
    nrm = lambda k, shape, scale: jax.random.normal(k, shape, f32) * scale
    gain = lambda k, shape: 1.0 + 0.05 * jax.random.normal(k, shape, f32)
    d = D_MODEL
    return {
        "x": jax.random.normal(ks[0], (BATCH, SEQ, d), f32),
        "mem": jax.random.normal(ks[1], (BATCH, MEM_LEN, d), f32),
        "g_mix": gain(ks[2], (DEPTH, d)),
        "w_in_a": nrm(ks[3], (N_A, d, 2 * CONV_CH + MEM_WIDTH), d ** -0.5),
        "b_glu": nrm(ks[4], (N_A, 2 * CONV_CH), 0.02),
        "w_dw_a": nrm(ks[5], (N_A, CONV_WIDTH, CONV_CH), CONV_WIDTH ** -0.5),
        "b_dw_a": nrm(ks[6], (N_A, CONV_CH), 0.02),
        "ln_g": gain(ks[7], (N_A, CONV_CH)),
        "ln_b": nrm(ks[8], (N_A, CONV_CH), 0.02),
        "g_kv": gain(ks[9], (d,)),
        "w_kvf": nrm(ks[10], (d, 2 * MIX_WIDTH + N_FOX_HEADS), d ** -0.5),
        "b_f": 2.0 + 0.5 * jax.random.normal(ks[11], (N_FOX_HEADS,), f32),
        "w_in_b": nrm(ks[12], (N_B, d, MIX_WIDTH + MEM_WIDTH), d ** -0.5),
        "g_mem": gain(ks[13], (d,)),
        "w_mem_kv": nrm(ks[14], (DEPTH, d, 2 * MEM_WIDTH), d ** -0.5),
        "w_out": nrm(ks[15], (DEPTH, d, d), d ** -0.5),
        "g_ffn": gain(ks[16], (DEPTH, d)),
        "w_up": nrm(ks[17], (DEPTH, d, 2 * D_FF), d ** -0.5),
        "w_dw_f": nrm(ks[18], (DEPTH, FFN_CONV_WIDTH, 2 * D_FF), FFN_CONV_WIDTH ** -0.5),
        "b_dw_f": nrm(ks[19], (DEPTH, 2 * D_FF), 0.02),
        "w_down": nrm(ks[20], (DEPTH, D_FF, d), D_FF ** -0.5),
        "g_final": gain(ks[21], (d,)),
    }

def first_block(x, mem, g_mix, w_in_a, b_glu, w_dw_a, b_dw_a, ln_g, ln_b, g_kv, w_kvf, b_f,
              w_in_b, g_mem, w_mem_kv, w_out, g_ffn, w_up, w_dw_f, b_dw_f, w_down, g_final):
    bsz, seq, _ = x.shape
    mem_n = rmsnorm(mem, g_mem)
    k_sh = v_sh = cum_logf = None
    for l in range(DEPTH):
        h = rmsnorm(x, g_mix[l])
        mem_k, mem_v = jnp.split(mem_n @ w_mem_kv[l], 2, axis=-1)
        if l < N_A:
            p = h @ w_in_a[l]
            u, q_mem = p[..., :2 * CONV_CH], p[..., 2 * CONV_CH:]
            mix = conformer_conv(u, b_glu[l], w_dw_a[l], b_dw_a[l], ln_g[l], ln_b[l])
        else:
            if l == N_A:
                hk = rmsnorm(x, g_kv)
                kvf = hk @ w_kvf
                k_sh = kvf[..., :MIX_WIDTH].reshape(bsz, seq, N_FOX_HEADS, HEAD_DIM)
                v_sh = kvf[..., MIX_WIDTH:2 * MIX_WIDTH].reshape(bsz, seq, N_FOX_HEADS, HEAD_DIM)
                f_logit = (kvf[..., 2 * MIX_WIDTH:] + b_f).astype(jnp.float32)
                cum_logf = jnp.cumsum(jax.nn.log_sigmoid(f_logit), axis=1).transpose(0, 2, 1)
            p = h @ w_in_b[l - N_A]
            q, q_mem = p[..., :MIX_WIDTH], p[..., MIX_WIDTH:]
            q = q.reshape(bsz, seq, N_FOX_HEADS, HEAD_DIM)
            mix = forgetting_attention(q, k_sh, v_sh, cum_logf).reshape(bsz, seq, MIX_WIDTH)
        mem_o = memory_attention(q_mem, mem_k, mem_v)
        x = x + jnp.concatenate([mix, mem_o], axis=-1) @ w_out[l]
        x = x + conv_ffn(rmsnorm(x, g_ffn[l]), w_up[l], w_dw_f[l], b_dw_f[l], w_down[l])
    return rmsnorm(x, g_final)


N_A_2 = DEPTH // 2
N_B_2 = DEPTH - N_A_2
PLE_DIM = 256
EPS = 1e-6
NEG = -1e30
BIG = 1e30

RET_HEADS = D_MODEL // 256
RET_QK_DIM = D_MODEL // RET_HEADS
RET_V_DIM = 2 * RET_QK_DIM
RET_QK_W = RET_HEADS * RET_QK_DIM
RET_V_W = RET_HEADS * RET_V_DIM
RET_CHUNK = 128
ROPE_BASE = 10000.0

NSA_DK = 128
NSA_DV = 128
NSA_W = 2 * D_MODEL
NSA_HEADS = NSA_W // NSA_DV
NSA_GROUPS = 4
NSA_HPG = NSA_HEADS // NSA_GROUPS
NSA_KV_W = NSA_GROUPS * NSA_DK
CMP_LEN = 32
CMP_STRIDE = 16
CMP_HIDDEN = 256
SEL_BLOCK = 64
N_SEL = 16
WIN = 512
Q_BLOCK = 128


def rmsnorm_2(x, g):
    xf = x.astype(jnp.float32)
    y = xf * lax.rsqrt(jnp.mean(xf * xf, axis=-1, keepdims=True) + EPS)
    return (y * g.astype(jnp.float32)).astype(x.dtype)

def rotary(x, pos):
    half = x.shape[-1] // 2
    inv = ROPE_BASE ** (-jnp.arange(half, dtype=jnp.float32) / half)
    ang = pos.astype(jnp.float32)[:, None] * inv[None, :]
    cos, sin = jnp.cos(ang), jnp.sin(ang)
    x1, x2 = x[..., :half], x[..., half:]
    return jnp.concatenate([x1 * cos - x2 * sin, x1 * sin + x2 * cos], axis=-1)

def retention_chunkwise(q, k, v):
    b, h, t, _ = q.shape
    nc = t // RET_CHUNK
    lg = jnp.log1p(-(2.0 ** (-5.0 - jnp.arange(h, dtype=jnp.float32))))
    pos = jnp.arange(RET_CHUNK, dtype=jnp.float32)
    diff = pos[:, None] - pos[None, :]
    decay = jnp.where(diff[None] >= 0,
                      jnp.exp(jnp.maximum(diff, 0.0)[None] * lg[:, None, None]), 0.0)
    q_dec = jnp.exp((pos + 1.0)[None, :] * lg[:, None])
    k_dec = jnp.exp((RET_CHUNK - 1.0 - pos)[None, :] * lg[:, None])
    chunk_dec = jnp.exp(RET_CHUNK * lg)

    def to_chunks(a):
        return jnp.moveaxis(a.reshape(b, h, nc, RET_CHUNK, a.shape[-1]), 2, 0)

    def step(state, qkv):
        qc, kc, vc = qkv
        s = jnp.einsum('bhnd,bhmd->bhnm', qc, kc) * decay
        o = (jnp.einsum('bhnm,bhmv->bhnv', s, vc)
             + jnp.einsum('bhnd,bhdv->bhnv', qc, state) * q_dec[..., None])
        state = (state * chunk_dec[:, None, None]
                 + jnp.einsum('bhmd,bhmv->bhdv', kc * k_dec[..., None], vc))
        return state, o

    state0 = jnp.zeros((b, h, q.shape[-1], v.shape[-1]), jnp.float32)
    _, o = lax.scan(step, state0, (to_chunks(q), to_chunks(k), to_chunks(v)))
    return jnp.moveaxis(o, 0, 2).reshape(b, h, t, v.shape[-1])

def retention_layer(h, g_norm, w_in, gn_gain, w_out):
    b, t, _ = h.shape
    proj = rmsnorm_2(h, g_norm) @ w_in
    q, k, v, gate = jnp.split(proj, [RET_QK_W, 2 * RET_QK_W, 2 * RET_QK_W + RET_V_W], axis=-1)

    def heads(a, d):
        return a.reshape(b, t, RET_HEADS, d).transpose(0, 2, 1, 3).astype(jnp.float32)

    pos = jnp.arange(t)
    q = rotary(heads(q, RET_QK_DIM), pos)
    k = rotary(heads(k, RET_QK_DIM), pos) * (RET_QK_DIM ** -0.5)
    o = retention_chunkwise(q, k, heads(v, RET_V_DIM))
    mu = jnp.mean(o, axis=-1, keepdims=True)
    var = jnp.mean(jnp.square(o - mu), axis=-1, keepdims=True)
    o = ((o - mu) * lax.rsqrt(var + EPS)).transpose(0, 2, 1, 3).reshape(b, t, RET_V_W)
    o = o * gn_gain.astype(jnp.float32)
    y = (jax.nn.silu(gate.astype(jnp.float32)) * o).astype(h.dtype) @ w_out
    return h + y

def per_layer_embedding(h, p_i, g, w_gate, w_emb):
    gate = jax.nn.sigmoid(rmsnorm_2(h, g) @ w_gate)
    return h + gate * (p_i @ w_emb)

def compress_blocks(a, pe, w1, w2):
    b, g, t, d = a.shape
    lc = CMP_LEN // CMP_STRIDE
    n_cmp = (t - CMP_LEN) // CMP_STRIDE + 1
    sub = a.reshape(b, g, t // CMP_STRIDE, CMP_STRIDE, d)
    blocks = jnp.concatenate([sub[:, :, o:o + n_cmp] for o in range(lc)], axis=3)
    blocks = (blocks + pe).reshape(b, g, n_cmp, CMP_LEN * d)
    return jax.nn.gelu(blocks @ w1) @ w2

def nsa_shared_kv(h, g_kv, w_kv, pe_k, w1_k, w2_k, pe_v, w1_v, w2_v):
    b, t, _ = h.shape
    proj = rmsnorm_2(h, g_kv) @ w_kv
    parts = proj.reshape(b, t, 6, NSA_GROUPS, NSA_DK).transpose(2, 0, 3, 1, 4)
    kc, vc, ks, vs, kw, vw = parts[0], parts[1], parts[2], parts[3], parts[4], parts[5]
    k_cmp = compress_blocks(kc, pe_k, w1_k, w2_k)
    v_cmp = compress_blocks(vc, pe_v, w1_v, w2_v)
    nslc = t // SEL_BLOCK
    k_sel = ks.reshape(b, NSA_GROUPS, nslc, SEL_BLOCK * NSA_DK)
    v_sel = vs.reshape(b, NSA_GROUPS, nslc, SEL_BLOCK * NSA_DV)
    pad = ((0, 0), (0, 0), (WIN, 0), (0, 0))
    return (k_cmp, v_cmp, k_sel, v_sel, jnp.pad(kw, pad), jnp.pad(vw, pad))

def selection_importance(p, nslc):
    f = SEL_BLOCK // CMP_STRIDE
    lc = CMP_LEN // CMP_STRIDE
    left = lc - 1
    right = f * nslc - p.shape[-1]
    pp = jnp.pad(p, ((0, 0), (0, 0), (0, 0), (left, right)))
    terms = []
    for o in range(-(lc - 1), f):
        w = float(min(o + lc, f) - max(o, 0))
        s = left + o
        terms.append(w * pp[..., s:s + f * (nslc - 1) + 1:f])
    return sum(terms[1:], terms[0])

def nsa_query_block(q, gates, blk, k_cmp, v_cmp, k_sel, v_sel, k_win, v_win):
    b = q.shape[0]
    scale = NSA_DK ** -0.5
    t = blk * Q_BLOCK + jnp.arange(Q_BLOCK)

    n_cmp = k_cmp.shape[2]
    cmp_end = jnp.arange(n_cmp) * CMP_STRIDE + CMP_LEN - 1
    valid_c = cmp_end[None, :] <= t[:, None]
    s_c = jnp.einsum('bgrqd,bgnd->bgrqn', q, k_cmp).astype(jnp.float32) * scale
    p_c = jnp.where(valid_c, jax.nn.softmax(jnp.where(valid_c, s_c, NEG), axis=-1), 0.0)
    o_c = jnp.einsum('bgrqn,bgnd->bgrqd', p_c, v_cmp.astype(jnp.float32))

    nslc = k_sel.shape[2]
    n_top = min(N_SEL, nslc)
    imp = selection_importance(jnp.sum(p_c, axis=2), nslc)
    cur = (t // SEL_BLOCK)[:, None]
    j = jnp.arange(nslc)[None, :]
    forced = (j == 0) | (j == cur) | (j == cur - 1)
    score = jnp.where(j <= cur, jnp.where(forced, BIG, imp), -BIG)
    top_v, top_i = lax.top_k(score, n_top)
    sel_ok = top_v > -0.5 * BIG
    idx = top_i.reshape(b, NSA_GROUPS, Q_BLOCK * n_top)
    bi = jnp.arange(b)[:, None, None]
    gi = jnp.arange(NSA_GROUPS)[None, :, None]
    ks = k_sel[bi, gi, idx].reshape(b, NSA_GROUPS, Q_BLOCK, n_top, SEL_BLOCK, NSA_DK)
    vs = v_sel[bi, gi, idx].reshape(b, NSA_GROUPS, Q_BLOCK, n_top, SEL_BLOCK, NSA_DV)
    kpos = top_i[..., None] * SEL_BLOCK + jnp.arange(SEL_BLOCK)
    valid_s = (sel_ok[..., None] & (kpos <= t[:, None, None]))[:, :, None]
    s_s = jnp.einsum('bgrqd,bgqnkd->bgrqnk', q, ks).astype(jnp.float32) * scale
    p_s = jnp.where(valid_s, jax.nn.softmax(jnp.where(valid_s, s_s, NEG), axis=(-2, -1)), 0.0)
    o_s = jnp.einsum('bgrqnk,bgqnkd->bgrqd', p_s, vs.astype(jnp.float32))

    start = blk * Q_BLOCK
    kw = lax.dynamic_slice_in_dim(k_win, start, WIN + Q_BLOCK, axis=2)
    vw = lax.dynamic_slice_in_dim(v_win, start, WIN + Q_BLOCK, axis=2)
    kwpos = start - WIN + jnp.arange(WIN + Q_BLOCK)
    valid_w = ((kwpos[None, :] <= t[:, None]) & (kwpos[None, :] > t[:, None] - WIN)
               & (kwpos[None, :] >= 0))
    s_w = jnp.einsum('bgrqd,bgkd->bgrqk', q, kw).astype(jnp.float32) * scale
    p_w = jax.nn.softmax(jnp.where(valid_w, s_w, NEG), axis=-1)
    o_w = jnp.einsum('bgrqk,bgkd->bgrqd', p_w, vw.astype(jnp.float32))

    return gates[..., 0:1] * o_c + gates[..., 1:2] * o_s + gates[..., 2:3] * o_w

def nsa_layer(h, g_norm, w_in, w_out, k_cmp, v_cmp, k_sel, v_sel, k_win, v_win):
    b, t, _ = h.shape
    proj = rmsnorm_2(h, g_norm) @ w_in
    q_w = NSA_HEADS * NSA_DK
    q, gate, bgate = jnp.split(proj, [q_w, q_w + NSA_W], axis=-1)
    nqb = t // Q_BLOCK
    qb = q.reshape(b, nqb, Q_BLOCK, NSA_GROUPS, NSA_HPG, NSA_DK).transpose(1, 0, 3, 4, 2, 5)
    gb = jax.nn.sigmoid(bgate.astype(jnp.float32)).reshape(
        b, nqb, Q_BLOCK, NSA_GROUPS, NSA_HPG, 3).transpose(1, 0, 3, 4, 2, 5)

    def body(args):
        q_blk, g_blk, blk = args
        return nsa_query_block(q_blk, g_blk, blk, k_cmp, v_cmp, k_sel, v_sel, k_win, v_win)

    o = lax.map(body, (qb, gb, jnp.arange(nqb)))
    o = o.transpose(1, 0, 4, 2, 3, 5).reshape(b, t, NSA_W)
    y = (jax.nn.silu(gate.astype(jnp.float32)) * o).astype(h.dtype) @ w_out
    return h + y

def second_inputs(seed: int = 0) -> dict:
    key = jax.random.key(seed)
    ks = jax.random.split(key, 24)

    def nrm(k, shape, scale):
        return jax.random.normal(k, shape, jnp.float32) * scale

    def gain(k, shape):
        return 1.0 + 0.02 * jax.random.normal(k, shape, jnp.float32)

    ret_in_w = 2 * RET_QK_W + 2 * RET_V_W
    nsa_in_w = NSA_HEADS * NSA_DK + NSA_W + 3 * NSA_HEADS
    return {
        "x": nrm(ks[0], (BATCH, SEQ, D_MODEL), 1.0),
        "p": nrm(ks[1], (DEPTH, BATCH, SEQ, PLE_DIM), 1.0),
        "ret_norm": gain(ks[2], (N_A_2, D_MODEL)),
        "ret_w_in": nrm(ks[3], (N_A_2, D_MODEL, ret_in_w), D_MODEL ** -0.5),
        "ret_gn": gain(ks[4], (N_A_2, RET_V_W)),
        "ret_w_out": nrm(ks[5], (N_A_2, RET_V_W, D_MODEL), RET_V_W ** -0.5),
        "kv_norm": gain(ks[6], (D_MODEL,)),
        "kv_w": nrm(ks[7], (D_MODEL, 6 * NSA_KV_W), D_MODEL ** -0.5),
        "cmp_pe_k": nrm(ks[8], (CMP_LEN, NSA_DK), 0.02),
        "cmp_w1_k": nrm(ks[9], (CMP_LEN * NSA_DK, CMP_HIDDEN), (CMP_LEN * NSA_DK) ** -0.5),
        "cmp_w2_k": nrm(ks[10], (CMP_HIDDEN, NSA_DK), CMP_HIDDEN ** -0.5),
        "cmp_pe_v": nrm(ks[11], (CMP_LEN, NSA_DV), 0.02),
        "cmp_w1_v": nrm(ks[12], (CMP_LEN * NSA_DV, CMP_HIDDEN), (CMP_LEN * NSA_DV) ** -0.5),
        "cmp_w2_v": nrm(ks[13], (CMP_HIDDEN, NSA_DV), CMP_HIDDEN ** -0.5),
        "nsa_norm": gain(ks[14], (N_B_2, D_MODEL)),
        "nsa_w_in": nrm(ks[15], (N_B_2, D_MODEL, nsa_in_w), D_MODEL ** -0.5),
        "nsa_w_out": nrm(ks[16], (N_B_2, NSA_W, D_MODEL), NSA_W ** -0.5),
        "ple_norm": gain(ks[17], (DEPTH, D_MODEL)),
        "ple_w_gate": nrm(ks[18], (DEPTH, D_MODEL, D_MODEL), D_MODEL ** -0.5),
        "ple_w_emb": nrm(ks[19], (DEPTH, PLE_DIM, D_MODEL), PLE_DIM ** -0.5),
        "final_norm": gain(ks[20], (D_MODEL,)),
    }

def second_block(x, p, ret_norm, ret_w_in, ret_gn, ret_w_out, kv_norm, kv_w,
              cmp_pe_k, cmp_w1_k, cmp_w2_k, cmp_pe_v, cmp_w1_v, cmp_w2_v,
              nsa_norm, nsa_w_in, nsa_w_out, ple_norm, ple_w_gate, ple_w_emb, final_norm):
    h = x
    shared = None
    for i in range(DEPTH):
        if i < N_A_2:
            h = retention_layer(h, ret_norm[i], ret_w_in[i], ret_gn[i], ret_w_out[i])
        else:
            if i == N_A_2:
                shared = nsa_shared_kv(h, kv_norm, kv_w, cmp_pe_k, cmp_w1_k, cmp_w2_k,
                                       cmp_pe_v, cmp_w1_v, cmp_w2_v)
            j = i - N_A_2
            h = nsa_layer(h, nsa_norm[j], nsa_w_in[j], nsa_w_out[j], *shared)
        h = per_layer_embedding(h, p[i], ple_norm[i], ple_w_gate[i], ple_w_emb[i])
    return rmsnorm_2(h, final_norm)


def setup_inputs(seed=0):
    out = dict(first_inputs(seed))
    for name, value in second_inputs(seed + 1).items():
        if name != "x":
            out[name + "_2"] = value
    return out


def reference(
    x, mem, g_mix, w_in_a, b_glu, w_dw_a, b_dw_a, ln_g, ln_b, g_kv, w_kvf, b_f, w_in_b, g_mem,
    w_mem_kv, w_out, g_ffn, w_up, w_dw_f, b_dw_f, w_down, g_final, p_2, ret_norm_2, ret_w_in_2,
    ret_gn_2, ret_w_out_2, kv_norm_2, kv_w_2, cmp_pe_k_2, cmp_w1_k_2, cmp_w2_k_2, cmp_pe_v_2,
    cmp_w1_v_2, cmp_w2_v_2, nsa_norm_2, nsa_w_in_2, nsa_w_out_2, ple_norm_2, ple_w_gate_2,
    ple_w_emb_2, final_norm_2,
):
    x = first_block(
        x, mem, g_mix, w_in_a, b_glu, w_dw_a, b_dw_a, ln_g, ln_b, g_kv, w_kvf, b_f, w_in_b,
        g_mem, w_mem_kv, w_out, g_ffn, w_up, w_dw_f, b_dw_f, w_down, g_final,
    )
    return second_block(
        x, p_2, ret_norm_2, ret_w_in_2, ret_gn_2, ret_w_out_2, kv_norm_2, kv_w_2, cmp_pe_k_2,
        cmp_w1_k_2, cmp_w2_k_2, cmp_pe_v_2, cmp_w1_v_2, cmp_w2_v_2, nsa_norm_2, nsa_w_in_2,
        nsa_w_out_2, ple_norm_2, ple_w_gate_2, ple_w_emb_2, final_norm_2,
    )


_drawn_inputs = setup_inputs


def setup_inputs(seed=0):
    import zlib

    import numpy as np

    out = dict(_drawn_inputs(seed))
    spreads = {}
    factors = {'b_glu': 3.452,
     'ln_b': 3.761,
     'g_mem': 8.0,
     'ret_norm_2': 3.12,
     'ret_gn_2': 6.287,
     'kv_norm_2': 8.0,
     'cmp_pe_k_2': 8.0,
     'cmp_pe_v_2': 60.202,
     'nsa_norm_2': 8.0,
     'ple_norm_2': 42.734,
     'final_norm_2': 7.985}
    for name, (base, spread) in spreads.items():
        noise = np.random.default_rng([zlib.crc32(name.encode()), seed]).standard_normal(out[name].shape)
        drawn = base * np.exp(spread * noise) if base else spread * noise
        out[name] = __import__('jax').numpy.asarray(drawn.astype(out[name].dtype))
    for name, factor in factors.items():
        out[name] = (out[name] * factor).astype(out[name].dtype)
    return out
```

```python
from contextlib import ExitStack

import numpy as np

import concourse.bass as bass
from concourse import mybir

F32 = mybir.dt.float32
F32R = mybir.dt.float32r
BF16 = mybir.dt.bfloat16
ALU = mybir.AluOpType
ACT = mybir.ActivationFunctionType
AX_X = mybir.AxisListType.X

P = 128
T = 256
TT = T // P
D = 1024
KD = D // P
DH = 64
MIX = 768
NMB = MIX // P
FOX = MIX // DH
CONV = 31
DFF = 2816
FSTEP = DFF // 256
RH = 4
NSA_H = 16
NSA_G = 4
CMP_L = 32
CMP_S = 16
NEG = -1e30
RING = 3
TILE_COLS = 2048
RMS_EPS = 1e-6
LN_EPS = 1e-5
GELU_C = 0.7978845608028654


def layout(parts):
    at, out = 0, {}
    for name, n in parts:
        out[name] = (at, at + n)
        at += n
    return out, at


PARAM_PARTS = [("g_mem", KD), ("g_mix0", KD), ("g_mix1", KD), ("g_ffn0", KD), ("g_ffn1", KD), ("g_kv", KD),
               ("ret_norm", KD), ("ple_norm0", KD), ("ple_norm1", KD), ("kv_norm", KD), ("nsa_norm", KD),
               ("b_glu", 2 * NMB), ("b_dw_a", NMB), ("ln_g", NMB), ("ln_b", NMB), ("w_dw_a", NMB * CONV),
               ("w_dw_f0", 44 * 3), ("w_dw_f1", 44 * 3), ("b_dw_f0", 44), ("b_dw_f1", 44), ("ret_gn", 16),
               ("pe_k", CMP_L), ("pe_v", CMP_L), ("w2_k", 2 * P), ("w2_v", 2 * P),
               ("w_f", KD * FOX), ("w_bg", KD * 48)]
PCOL, N_PARAM = layout(PARAM_PARTS)
CONST_PARTS = [("ident", P), ("cossin", 2 * T), ("sincos", 2 * T), ("decay", RH * 384), ("tri8", TT * T),
               ("causal", P), ("cmpmask", TT * CMP_S), ("rowvalid", TT), ("ones", P)]
CCOL, N_CONST = layout(CONST_PARTS)


def plan_tiles():
    t = []
    for l in range(2):
        t += [("mk", l), ("mv", l)]
    for j in range(3):
        t += [("ca", j), ("cg", j)]
    t += [("qm", 0)] + [("o0", c) for c in range(4)]

    def ffn(l):
        out = [("fg", l, 0), ("fv", l, 0)]
        for s in range(1, FSTEP):
            out += [("fg", l, s), ("fv", l, s), ("fd", l, s - 1)]
        return out + [("fd", l, FSTEP - 1)]

    t += ffn(0)
    t += [("v1", j) for j in range(3)] + [("k1", j) for j in range(3)] + [("q1", j) for j in range(3)]
    t += [("qm", 1)] + [("o1", c) for c in range(4)]
    t += ffn(1)
    for h in range(RH):
        t += [("rq", h), ("rk", h)]
    for h in range(RH):
        t += [("rv", h, 0), ("rv", h, 1), ("rg", h, 0), ("rg", h, 1)]
    t += [("ro", c) for c in range(8)]
    t += [("pe", 0)] + [("pg0", c) for c in range(4)]
    for n in ("kc", "vc", "ks", "kw"):
        t += [(n, j) for j in range(2)]
    for n in ("vs", "vw"):
        t += [(n, j) for j in range(2)]
    t += [("c1k", j) for j in range(4)] + [("c1v", j) for j in range(4)]
    for j in range(8):
        t += [("nq", j), ("ng", j)]
    t += [("no", c) for c in range(8)]
    t += [("pe", 1)] + [("pg1", c) for c in range(4)]
    return t


TILES = plan_tiles()
TILE = {key: n for n, key in enumerate(TILES)}


def plan_banks():
    u = []

    def gemm(key, freer, last=None):
        u.append(("A", key, freer, last or key))

    def aux(ring, key, freer):
        u.append((ring, key, freer, None))

    def norm(n):
        for j in range(4):
            aux("A", ("tr", n, j), "dve")

    def acc(key, last):
        for i in range(4):
            u.append(("B", (key, i), "dve", last))

    def attention(base, n):
        for s in range(n + 2):
            if s < n:
                aux("B", ("S", base + s), "act")
            if 0 <= s - 1 < n:
                aux("B", ("T", base + s - 1), "dve")
            if 0 <= s - 2 < n:
                if (s - 2) % 2 == 0:
                    u.append(("B", ("O", base + s - 2), "dve_values", "later"))
                else:
                    u.append(("complete", ("O", base + s - 3), None, None))

    def ffn(l):
        u.extend(("B", (f"f{l}", i), "dve", ("fd", l, FSTEP - 1)) for i in range(4))
        for s in range(FSTEP):
            gemm(("fg", l, s), "dve")
            gemm(("fv", l, s), "dve")

    norm(0)
    for l in range(2):
        gemm(("mk", l), "act")
        gemm(("mv", l), "act")
    norm(1)
    for j in range(3):
        gemm(("ca", j), "act")
        gemm(("cg", j), "act")
    gemm(("qm", 0), "act")
    attention(0, 4)
    aux("B", ("mean",), "dve")
    aux("B", ("var",), "dve")
    acc("o0", ("o0", 3))
    norm(2)
    ffn(0)
    norm(3)
    for j in range(3):
        gemm(("v1", j), "act")
    for j in range(3):
        gemm(("k1", j), "act")
    for j in range(3):
        gemm(("q1", j), "act")
    gemm(("qm", 1), "act")
    aux("A", ("fl",), "dve")
    aux("A", ("cum",), "dve")
    attention(4, 16)
    acc("o1", ("o1", 3))
    norm(4)
    ffn(1)
    norm(5)
    for h in range(RH):
        gemm(("rq", h), "dve")
        gemm(("rk", h), "dve")
    for h in range(RH):
        for i in range(TT):
            gemm(("rv", h, i, "out"), "act", ("rv", h, 1))
        for i in range(TT):
            gemm(("rg", h, i, "out"), "dve", ("rg", h, 1))
        aux("B", ("rs", h), "dve")
        for i in range(TT):
            aux("B", ("ro", h, i), "dve")
        if h:
            for j in range(2):
                aux("A", ("ry", h - 1, j), "dve")
    for j in range(2):
        aux("A", ("ry", RH - 1, j), "dve")
    acc("ro", ("ro", 7))
    ple(u, norm, acc, 0, 6)
    norm(7)
    for n in ("kc", "vc", "ks", "kw"):
        for j in range(2):
            gemm((n, j), "act")
    for n in ("vs", "vw"):
        for i in range(TT):
            gemm((n, i, "out"), "act", (n, 1))
    aux("A", ("bg",), "act")
    u.append(("B", ("hk",), "act", ("c1k", 3)))
    u.append(("B", ("hv",), "act", ("c1v", 3)))
    aux("B", ("ht",), "act")
    aux("B", ("kct",), "act")
    aux("B", ("vcm",), "act")
    gemm(("nq", 0), "act")
    gemm(("ng", 0), "dve")
    for s in range(NSA_H + 2):
        if s < NSA_H:
            aux("B", ("Ss", s), "act")
            aux("B", ("Sw", s), "act")
        if 0 <= s - 1 < NSA_H:
            aux("A", ("Ts", s - 1), "dve")
            aux("A", ("Tw", s - 1), "act")
        if s // 2 + 1 < 8:
            if s % 2 == 0:
                gemm(("nq", s // 2 + 1), "act")
            else:
                gemm(("ng", s // 2 + 1), "dve")
        if 0 <= s - 2 < NSA_H:
            aux("B", ("On", s - 2), "dve")
    acc("no", ("no", 7))
    ple(u, norm, acc, 1, 8)
    return u


def ple(u, norm, acc, l, n):
    u.append(("A", ("pt", l), "dve", None))
    norm(n)
    for i in range(4):
        u.append(("A", ("pe", l, i), "dve", ("pe", l)))
    acc(f"pg{l}", (f"pg{l}", 3))


BANKS = plan_banks()


class Uses:

    def __init__(self):
        at = {"A": 0, "B": 0}
        freed = {}
        history = {"A": [], "B": []}
        aux = 0
        self.bank, self.ready, self.freed, self.before = {}, {}, {}, {}
        for ring, key, freer, last in BANKS:
            if ring == "complete":
                aux += 1
                self.ready[key] = ("aux", aux)
                continue
            assert key not in self.bank, key
            n = at[ring]
            at[ring] += 1
            self.bank[key] = (4 if ring == "A" else 0) + n % 4
            who = (ring, freer)
            freed[who] = freed.get(who, 0) + 1
            self.freed[key] = (who, freed[who])
            self.before[key] = self.freed[history[ring][-4]] if n >= 4 else None
            history[ring].append(key)
            if last is None:
                aux += 1
                self.ready[key] = ("aux", aux)
            elif last != "later":
                self.ready[key] = ("tile", TILE[last] + 1)


USES = Uses()


class After:

    def __init__(self, sem):
        self.sem, self.n = sem, 0

    def next(self, k=1):
        self.n += k
        return self.sem, self.n


def program(nc, wstream, params, consts, x_in, mem_in, p_in, b_f, g_final, final_norm, out):
    NT = len(TILES)
    with ExitStack() as ctx:
        def sb(name, shape, dt=F32):
            return ctx.enter_context(nc.sbuf_tensor(name, shape, dt))

        def sem(name):
            return ctx.enter_context(nc.semaphore(name))

        RAW = sb("RAW", [P, RING, TILE_COLS])
        WH = sb("WH", [P, RING, TILE_COLS], F32R)
        WL = sb("WL", [P, RING, TILE_COLS], F32R)
        XH = sb("XH", [P, KD, T], F32R)
        XL = sb("XL", [P, KD, T], F32R)
        MH = sb("MH", [P, 16, T], F32R)
        ML = sb("ML", [P, 16, T], F32R)
        SWH = sb("SWH", [P, KD * (FOX + 48)], F32R)
        SWL = sb("SWL", [P, KD * (FOX + 48)], F32R)
        PH = sb("PH", [P, 2, T], F32R)
        PL = sb("PL", [P, 2, T], F32R)
        x = sb("x", [P, TT, D])
        xn = sb("xn", [P, TT, D])
        par = sb("par", [P, N_PARAM])
        con = sb("con", [P, N_CONST])
        gfree = sb("gfree", [P, D])
        bfree = sb("bfree", [P, FOX])
        junk = sb("junk", [P, D], BF16)
        mkt = sb("mkt", [P, 2, 2, T])
        mvv = sb("mvv", [P, 2, TT, T])
        identb = sb("identb", [P, P], BF16)
        causb = sb("causb", [P, P], BF16)
        cmpb = sb("cmpb", [P, TT * CMP_S], BF16)
        hbglu = sb("hbglu", [P, 2 * NMB])
        hgn = sb("hgn", [P, 16])
        eps = sb("eps", [P, 2])
        mhalf = sb("mhalf", [P, 2])
        ss = sb("ss", [P, 11, TT])
        rstd = sb("rstd", [P, 11, TT])
        stat = sb("stat", [P, 80])
        WORK = 10912
        work = sb("work", [P, WORK])
        bank = [ctx.enter_context(nc.psum_tensor(f"bank{i}", [P, 512], F32)) for i in range(8)]

        def col(name, i=None, n=1):
            a, b = PCOL[name]
            return par[:, a:b] if i is None else par[:, a + i:a + i + n]

        def const(name):
            a, b = CCOL[name]
            return con[:, a:b]

        ident = const("ident")
        ones = const("ones")

        def wk(at, *shape):
            n = int(np.prod(shape))
            assert at + n <= WORK, (at, n)
            v = work[:, at:at + n]
            if len(shape) == 2:
                v = v.rearrange("p (a b) -> p a b", a=shape[0])
            if len(shape) == 3:
                v = v.rearrange("p (a b c) -> p a b c", a=shape[0], b=shape[1])
            return v

        memx = wk(0, TT, D)
        q_mem = wk(0, 2, T)
        q1 = wk(512, NMB, T)
        k1 = wk(2048, NMB, T)
        v1 = wk(3584, TT, MIX)
        prob = wk(5120, 2, 512)
        probT = wk(6144, 2, 512)
        cumT = wk(7168, 2, T)
        lf = wk(7680, 4, TT * FOX)
        vpad = wk(512, NMB, CONV - 1 + T)
        conv = wk(2304, NMB, T)
        lnsq = wk(3840, NMB, T)
        rs_ln = wk(7168, T)
        glu_a = wk(7424, 2, T)
        glu_t = wk(7936, 2, T)
        z = wk(8448, NMB, T)
        fy = wk(0, 2, 4 * T)
        fth = wk(2048, 2, 2 * T)
        fa = wk(3072, 2, 2 * T)
        qr = wk(0, RH, 2 * T)
        kr = wk(2048, RH, 2 * T)
        rm = wk(4096, 2, 2 * T)
        sdt = wk(5120, 2, 384)
        rv = wk(5888, TT, 512)
        rth = wk(6912, TT, 512)
        rgs = wk(7936, TT, 512)
        ry = wk(8960, TT, 512)
        pin = wk(10400, TT, T)
        pth = wk(512, 4, 512)
        ksT = wk(0, NSA_G, T)
        kwT = wk(1024, NSA_G, T)
        vs = wk(2048, TT, 512)
        vw = wk(3072, TT, 512)
        kct = wk(4096, 64)
        vcm = wk(4160, NSA_G, P)
        g3 = wk(4672, TT, 48)
        kvc = wk(4768, 8, T)
        blocks = wk(6816, CMP_L, P)
        hx = wk(4768, T)
        hs = wk(5024, T)
        hth = wk(5280, T)
        hT = wk(5536, 2, P)
        qb = wk(4768, 2, 2 * T)
        nth = wk(5792, 2 * T)
        gs = wk(6304, 2, 2 * T)
        pS = wk(7328, 2, 384)
        pW = wk(8096, 2, 384)
        pC = wk(8864, 2, TT * CMP_S)
        ptS = wk(8928, 384)
        ptW = wk(9312, 384)
        ptC = wk(9696, T)
        om = xn[:, 0, 0:2 * T].rearrange("p (e t) -> p e t", e=2)

        w_loaded = [sem(f"w_loaded{i}") for i in range(RING)]
        w_rounded = sem("w_rounded")
        w_split = sem("w_split")
        w_used = sem("w_used")
        aux_done = sem("aux_done")
        freed = {(r, e): sem(f"freed_{r}_{e}") for r in "AB" for e in ("act", "dve", "dve_values")}
        small_loaded = sem("small_loaded")
        x_loaded = sem("x_loaded")
        mem_loaded = sem("mem_loaded")
        p_loaded = sem("p_loaded")
        gf_loaded = sem("gf_loaded")
        prepared = sem("prepared")
        pool_const = sem("pool_const")
        sw_rounded = sem("sw_rounded")
        sw_split = sem("sw_split")
        sq_done = sem("sq_done")
        ms_done = sem("ms_done")
        rstd_done = sem("rstd_done")
        xn_done = sem("xn_done")
        x_new = sem("x_new")
        hi_done = sem("hi_done")
        lo_done = sem("lo_done")
        act_for_pe = sem("act_for_pe")
        act_for_dve = sem("act_for_dve")
        dve_for_pe = sem("dve_for_pe")
        dve_for_act = sem("dve_for_act")
        dve_chain = sem("dve_chain")
        act_chain = sem("act_chain")
        max_done = sem("max_done")
        exp_done = sem("exp_done")
        prob_done = sem("prob_done")
        pt_done = sem("pt_done")
        gn_stat = sem("gn_stat")
        gn_rstd = sem("gn_rstd")
        out_done = sem("out_done")
        out_stored = sem("out_stored")

        def ready(eng, key):
            kind, n = USES.ready[key]
            eng.wait_ge(aux_done if kind == "aux" else w_used, n)

        def is_free(eng, key):
            who, n = USES.freed[key]
            eng.wait_ge(freed[who], n)

        order = {"act": {}, "dve": {}}

        def free(ins, key, eng):
            who, n = USES.freed[key]
            assert who[1].split("_")[0] == eng, key
            order[eng][who] = order[eng].get(who, 0) + 1
            assert order[eng][who] == n, (key, n, order[eng][who])
            ins.then_inc(freed[who], 1)

        def B(key):
            return bank[USES.bank[key]]

        norms = {0: ["g_mem"], 1: ["g_mix0"], 2: ["g_ffn0"], 3: ["g_mix1", "g_kv"], 4: ["g_ffn1"], 5: ["ret_norm"],
                 6: ["ple_norm0"], 7: ["nsa_norm", "kv_norm"], 8: ["ple_norm1"]}
        x_versions = {1: 0, 2: 2, 3: 4, 4: 6, 9: 8, 5: 10, 6: 12, 7: 14, 8: 16, 10: 18}

        block = ctx.enter_context(nc.Block())

        @block.sync
        def _(sp):
            sp.dma_start(memx, mem_in.rearrange("o (i p) d -> p (o i) d", p=P)).then_inc(mem_loaded, 16)
            sp.dma_start(par[:, :], params).then_inc(small_loaded, 16)
            sp.dma_start(con[:, :], consts).then_inc(small_loaded, 16)

            def load(t):
                if t >= RING:
                    sp.wait_ge(w_split, t - RING + 1)
                sp.dma_start(RAW[:, t % RING, :], wstream[t]).then_inc(w_loaded[t % RING], 16)

            for t in range(RING):
                load(t)
            sp.dma_start(x[:, :, :], x_in.rearrange("o (i p) d -> p (o i) d", p=P)).then_inc(x_loaded, 16)
            sp.dma_start(bfree[:, :], b_f.partition_broadcast(P)).then_inc(small_loaded, 16)
            sp.dma_start(gfree[:, :], g_final.partition_broadcast(P)).then_inc(gf_loaded, 16)
            sp.dma_start(pin, p_in[0].rearrange("o (i p) d -> p (o i) d", p=P)).then_inc(p_loaded, 16)
            for t in range(RING, NT):
                if TILES[t] == ("ro", 0):
                    sp.wait_ge(x_new, 10)
                    sp.dma_start(gfree[:, :], final_norm.partition_broadcast(P)).then_inc(gf_loaded, 16)
                if TILES[t] == ("nq", 3):
                    sp.wait_ge(w_used, TILE[("c1k", 0)] + 1)
                    sp.dma_start(pin, p_in[1].rearrange("o (i p) d -> p (o i) d", p=P)).then_inc(p_loaded, 16)
                load(t)
            for i in range(TT):
                sp.wait_ge(out_done, i + 1)
                sp.dma_start(out[0, i * P:(i + 1) * P, :], xn[:, i, :]).then_inc(out_stored, 16)
            sp.wait_ge(out_stored, 16 * TT)

        @block.gpsimd
        def _(pool):
            sq, ms = After(sq_done), After(ms_done)
            gn = After(gn_stat)
            nc.gpsimd.memset(mhalf[:, :], -0.5).then_inc(pool_const, 1)
            pool.wait_ge(pool_const, 1)

            def rms(n):
                pool.wait_ge(*sq.next(TT))
                nc.gpsimd.tensor_scalar(ss[:, n, :], ss[:, n, :], 1.0 / D, RMS_EPS, ALU.mult, ALU.add).then_inc(ms_done, 1)
                pool.wait_ge(*ms.next())
                nc.gpsimd.tensor_tensor(rstd[:, n, :], ss[:, n, :], mhalf[:, :], ALU.pow).then_inc(rstd_done, 1)

            for n in (0, 1, 2, 3, 4, 9, 5):
                rms(n)
            for h in range(RH):
                a = 16 + 4 * (h % 2)
                pool.wait_ge(*gn.next())
                nc.gpsimd.tensor_tensor(stat[:, a + 2:a + 4], stat[:, a:a + 2], mhalf[:, :], ALU.pow).then_inc(gn_rstd, 1)
            for n in (6, 7, 8, 10):
                rms(n)

        @block.tensor
        def _(pe):
            tiles, uses = [0], [0]
            xn_a, hi_a, lo_a = After(xn_done), After(hi_done), After(lo_done)
            act_a, dve_a = After(act_for_pe), After(dve_for_pe)
            prob_a, pt_a = After(prob_done), After(pt_done)
            mm = nc.tensor.matmul

            def take(key):
                while BANKS[uses[0]][0] == "complete":
                    uses[0] += 1
                assert BANKS[uses[0]][1] == key, (BANKS[uses[0]], key)
                uses[0] += 1
                if USES.before[key]:
                    who, n = USES.before[key]
                    pe.wait_ge(freed[who], n)
                return B(key)

            def tile(key):
                t = tiles[0]
                assert TILES[t] == key, (TILES[t], key)
                tiles[0] += 1
                pe.wait_ge(w_split, t + 1)
                return WH[:, t % RING, :], WL[:, t % RING, :]

            def three(o, wide, a, b, start, stop):
                (ah, al), (bh, bl) = a, b
                mm(o, ah, bh, start=start, stop=False)
                mm(o, ah, bl, start=False, stop=False)
                return mm(o, al, bh, start=False, stop=stop)

            def gemm_t(key, xh, xl):
                o = take(key)
                wh, wl = tile(key)
                for b in range(2):
                    for k in range(KD):
                        s = slice(k * 256 + b * P, k * 256 + b * P + P)
                        last = three(o[:, b * T:(b + 1) * T], T, (wh[:, s], wl[:, s]), (xh[:, k, :], xl[:, k, :]),
                                     k == 0, k == KD - 1)
                last.then_inc(w_used, 1)

            def gemm_v(key, xh, xl):
                o = take(key)
                wh, wl = tile(key)
                for i in range(TT):
                    for k in range(KD):
                        s, c = slice(i * P, (i + 1) * P), slice(k * 256, (k + 1) * 256)
                        last = three(o[:, i * 256:(i + 1) * 256], 256, (xh[:, k, s], xl[:, k, s]), (wh[:, c], wl[:, c]),
                                     k == 0, k == KD - 1)
                last.then_inc(w_used, 1)

            def gemm_n(name, xh, xl):
                o = [take((*name, i, "out")) for i in range(TT)]
                for half in range(2):
                    wh, wl = tile((*name, half))
                    for i in range(TT):
                        for k in range(4):
                            kk, s, c = half * 4 + k, slice(i * P, (i + 1) * P), slice(k * 512, (k + 1) * 512)
                            last = three(o[i][:, :], 512, (xh[:, kk, s], xl[:, kk, s]), (wh[:, c], wl[:, c]),
                                         kk == 0, kk == KD - 1)
                    last.then_inc(w_used, 1)

            def gemm_d(key, o, xh, xl, k0, first, end):
                wh, wl = tile(key)
                for k in range(2):
                    for i in range(TT):
                        for half in range(2):
                            s, c = slice(i * P, (i + 1) * P), slice(k * D + half * 512, k * D + half * 512 + 512)
                            last = three(o[2 * i + half][:, :], 512, (xh[:, k0 + k, s], xl[:, k0 + k, s]),
                                         (wh[:, c], wl[:, c]), first and k == 0, end and k == 1)
                last.then_inc(w_used, 1)

            def norm(n):
                pe.wait_ge(*xn_a.next(TT))
                for j in range(4):
                    o = take(("tr", n, j))
                    for kk in range(2):
                        for i in range(TT):
                            last = nc.tensor.transpose(o[:, kk * T + i * P:kk * T + (i + 1) * P],
                                                       xn[:, i, (2 * j + kk) * P:(2 * j + kk + 1) * P], ident)
                    last.then_inc(aux_done, 1)
                is_free(pe, ("tr", n, 3))

            def attention(base, units, score, value):
                n = len(units)
                for s in range(n + 2):
                    if s < n:
                        o = take(("S", base + s))
                        score(units[s], o).then_inc(aux_done, 1)
                    if 0 <= s - 1 < n:
                        o = take(("T", base + s - 1))
                        pe.wait_ge(*prob_a.next())
                        p = prob[:, (s - 1) % 2, :]
                        kind = units[s - 1][0]
                        pieces = ([(0, 0), (256, 128), (128, 256), (384, 384)] if kind == "mem"
                                  else [(0, 0), (128, 128), (256, 256)])
                        for a, b in pieces:
                            last = nc.tensor.transpose(o[:, b:b + P], p[:, a:a + P], ident)
                        last.then_inc(aux_done, 1)
                    if 0 <= s - 2 < n:
                        if (s - 2) % 2 == 0:
                            o_val = take(("O", base + s - 2))
                        pe.wait_ge(*pt_a.next())
                        last = value(units[s - 2], o_val, probT[:, (s - 2) % 2, :])
                        if (s - 2) % 2 == 1:
                            last.then_inc(aux_done, 1)

            def score(unit, o):
                kind, h = unit[0], unit[-1]
                r = slice(DH * (h % 2), DH * (h % 2) + DH)
                if kind == "mem":
                    l = unit[1]
                    for i in range(TT):
                        last = mm(o[:, i * T:(i + 1) * T], q_mem[r, h // 2, i * P:(i + 1) * P], mkt[r, l, h // 2, :],
                                  start=True, stop=True)
                    return last
                for i in range(TT):
                    a, n = (0, P) if i == 0 else (P, T)
                    t = slice(i * P, (i + 1) * P)
                    mm(o[:, a:a + n], q1[r, h // 2, t], k1[r, h // 2, 0:n], start=True, stop=False)
                    mm(o[:, a:a + n], cumT[0:FOX, 0, t], ident[0:FOX, h:h + 1].to_broadcast([FOX, n]),
                       start=False, stop=False)
                    mm(o[:, a:a + n], ident[0:FOX, h:h + 1].to_broadcast([FOX, P]), cumT[0:FOX, 1, 0:n],
                       start=False, stop=False)
                    last = mm(o[:, a + n - P:a + n], identb[:, :], causb[:, :], start=False, stop=True)
                return last

            def value(unit, o, pt):
                kind, h = unit[0], unit[-1]
                r = slice(DH * (h % 2), DH * (h % 2) + DH)
                if kind == "mem":
                    l = unit[1]
                    for j in range(TT):
                        last = mm(o[r, 0:T], mvv[:, l, j, DH * h:DH * (h + 1)], pt[:, j * T:(j + 1) * T],
                                  start=(j == 0), stop=(j == TT - 1))
                    return last
                mm(o[r, 0:T], v1[:, 0, DH * h:DH * (h + 1)], pt[:, 0:T], start=True, stop=False)
                return mm(o[r, P:T], v1[:, 1, DH * h:DH * (h + 1)], pt[:, T:384], start=False, stop=True)

            def ffn(l):
                o = [take((f"f{l}", i)) for i in range(4)]
                for s in range(FSTEP + 1):
                    if s < FSTEP:
                        gemm_t(("fg", l, s), XH, XL)
                        gemm_t(("fv", l, s), XH, XL)
                    if s:
                        pe.wait_ge(*lo_a.next())
                        gemm_d(("fd", l, s - 1), o, MH, ML, 2 * ((s - 1) % 2), s == 1, s == FSTEP)

            def ple(l):
                o = take(("pt", l))
                pe.wait_ge(p_loaded, 16 * (l + 1))
                for k in range(2):
                    for i in range(TT):
                        last = nc.tensor.transpose(o[:, k * T + i * P:k * T + (i + 1) * P], pin[:, i, k * P:(k + 1) * P], ident)
                last.then_inc(aux_done, 1)
                norm(6 + 2 * l)
                o = [take(("pe", l, i)) for i in range(4)]
                gemm_d(("pe", l), o, PH, PL, 0, True, True)
                o = [take((f"pg{l}", i)) for i in range(4)]
                for c in range(4):
                    gemm_d((f"pg{l}", c), o, XH, XL, 2 * c, c == 0, c == 3)

            pe.wait_ge(small_loaded, 48)
            pe.wait_ge(prepared, 1)
            norm(0)
            for l in range(2):
                gemm_t(("mk", l), XH, XL)
                gemm_v(("mv", l), XH, XL)
            norm(1)
            for j in range(3):
                gemm_t(("ca", j), XH, XL)
                gemm_t(("cg", j), XH, XL)
            gemm_t(("qm", 0), XH, XL)
            pe.wait_ge(*act_a.next())
            attention(0, [("mem", 0, h) for h in range(4)], score, value)
            o = take(("mean",))
            pe.wait_ge(*dve_a.next())
            for b in range(NMB):
                last = mm(o[:, 0:T], ones, conv[:, b, :], start=(b == 0), stop=(b == NMB - 1))
            last.then_inc(aux_done, 1)
            o = take(("var",))
            pe.wait_ge(*act_a.next())
            for b in range(NMB):
                last = mm(o[:, 0:T], ones, lnsq[:, b, :], start=(b == 0), stop=(b == NMB - 1))
            last.then_inc(aux_done, 1)
            o = [take(("o0", i)) for i in range(4)]
            pe.wait_ge(*lo_a.next())
            for c in range(4):
                gemm_d(("o0", c), o, MH, ML, 2 * c, c == 0, c == 3)
            norm(2)
            ffn(0)
            norm(3)
            for j in range(3):
                gemm_v(("v1", j), MH, ML)
            for j in range(3):
                gemm_t(("k1", j), MH, ML)
            for j in range(3):
                gemm_t(("q1", j), XH, XL)
            gemm_t(("qm", 1), XH, XL)
            o = take(("fl",))
            pe.wait_ge(sw_split, 1)
            for i in range(TT):
                for k in range(KD):
                    s, c = slice(i * P, (i + 1) * P), slice(k * FOX, (k + 1) * FOX)
                    last = three(o[:, i * FOX:(i + 1) * FOX], FOX, (MH[:, k, s], ML[:, k, s]), (SWH[:, c], SWL[:, c]),
                                 k == 0, k == KD - 1)
            last.then_inc(aux_done, 1)
            o = take(("cum",))
            pe.wait_ge(*dve_a.next())
            tri = const("tri8").rearrange("p (i t) -> p i t", i=TT)
            for i in range(TT):
                last = mm(o[0:FOX, 0:T], lf[:, 3, i * FOX:(i + 1) * FOX], tri[:, i, :], start=(i == 0), stop=(i == TT - 1))
            last.then_inc(aux_done, 1)
            pe.wait_ge(*act_a.next())
            pe.wait_ge(*dve_a.next())
            attention(4, [("fox", h) for h in range(FOX)] + [("mem", 1, h) for h in range(4)], score, value)
            o = [take(("o1", i)) for i in range(4)]
            pe.wait_ge(*lo_a.next())
            for c in range(4):
                gemm_d(("o1", c), o, MH, ML, 2 * c, c == 0, c == 3)
            norm(4)
            ffn(1)
            norm(5)
            for h in range(RH):
                gemm_t(("rq", h), XH, XL)
                gemm_t(("rk", h), XH, XL)

            def ret_turn(h):
                pe.wait_ge(*dve_a.next())
                for j in range(2):
                    o = take(("ry", h, j))
                    for kk in range(2):
                        for i in range(TT):
                            c = (2 * j + kk) * P
                            last = nc.tensor.transpose(o[:, kk * T + i * P:kk * T + (i + 1) * P], ry[:, i, c:c + P], ident)
                    last.then_inc(aux_done, 1)

            for h in range(RH):
                gemm_n(("rv", h), XH, XL)
                gemm_n(("rg", h), XH, XL)
                o = take(("rs", h))
                if h == 0:
                    pe.wait_ge(*dve_a.next())
                for m in range(TT):
                    for c in range(2):
                        last = mm(o[:, m * T:m * T + T - m * P], kr[:, h, c * T + m * P:c * T + (m + 1) * P],
                                  qr[:, h, c * T + m * P:(c + 1) * T], start=(c == 0), stop=(c == 1))
                last.then_inc(aux_done, 1)
                is_free(pe, ("rs", h))
                is_free(pe, ("rv", h, 1, "out"))
                for i in range(TT):
                    o = take(("ro", h, i))
                    for m in range(i + 1):
                        a = m * T + (i - m) * P
                        last = mm(o[:, :], sdt[:, h % 2, a:a + P], rv[:, m, :], start=(m == 0), stop=(m == i))
                    last.then_inc(aux_done, 1)
                if h:
                    ret_turn(h - 1)
            ret_turn(RH - 1)
            o = [take(("ro", i)) for i in range(4)]
            is_free(pe, ("ry", RH - 1, 1))
            for c in range(8):
                gemm_d(("ro", c), o, MH, ML, 2 * c, c == 0, c == 7)
            ple(0)
            norm(7)
            for n in ("kc", "vc", "ks", "kw"):
                for j in range(2):
                    gemm_t((n, j), MH, ML)
            for n in ("vs", "vw"):
                gemm_n((n,), MH, ML)
            o = take(("bg",))
            for i in range(TT):
                for k in range(KD):
                    s, c = slice(i * P, (i + 1) * P), slice(KD * FOX + k * 48, KD * FOX + (k + 1) * 48)
                    last = three(o[:, i * 48:(i + 1) * 48], 48, (XH[:, k, s], XL[:, k, s]), (SWH[:, c], SWL[:, c]),
                                 k == 0, k == KD - 1)
            last.then_inc(aux_done, 1)
            pe.wait_ge(*lo_a.next())
            bh = MH[:, :, :].rearrange("p a b -> p (a b)").rearrange("p (l c) -> p l c", c=P)
            bl = ML[:, :, :].rearrange("p a b -> p (a b)").rearrange("p (l c) -> p l c", c=P)
            for n, u in (("c1k", "hk"), ("c1v", "hv")):
                o = take((u,))
                for j in range(4):
                    wh, wl = tile((n, j))
                    for i in range(8):
                        l, c = 8 * j + i, slice(i * 256, (i + 1) * 256)
                        last = three(o[:, 0:256], 256, (bh[:, l, :], bl[:, l, :]), (wh[:, c], wl[:, c]), l == 0, l == CMP_L - 1)
                    last.then_inc(w_used, 1)
            o = take(("ht",))
            pe.wait_ge(*dve_a.next())
            for j in range(2):
                last = nc.tensor.transpose(o[:, j * P:(j + 1) * P], hs[:, j * P:(j + 1) * P], ident)
            last.then_inc(aux_done, 1)
            o = take(("kct",))
            is_free(pe, ("ht",))
            w2k, w2v = col("w2_k"), col("w2_v")
            for j in range(2):
                last = mm(o[:, 0:64], w2k[:, j * P:(j + 1) * P], hT[:, j, 0:64], start=(j == 0), stop=(j == 1))
            last.then_inc(aux_done, 1)
            o = take(("vcm",))
            for g in range(NSA_G):
                for j in range(2):
                    last = mm(o[0:CMP_S, g * P:(g + 1) * P], hT[:, j, 64 + g * CMP_S:64 + (g + 1) * CMP_S],
                              w2v[:, j * P:(j + 1) * P], start=(j == 0), stop=(j == 1))
            last.then_inc(aux_done, 1)
            is_free(pe, ("vcm",))
            gemm_t(("nq", 0), XH, XL)
            gemm_t(("ng", 0), XH, XL)
            for s in range(NSA_H + 2):
                if s < NSA_H:
                    h, g, qh = s, s // 4, qb[:, (s // 2) % 2, (s % 2) * T:(s % 2) * T + T]
                    oS, oW = take(("Ss", s)), take(("Sw", s))
                    is_free(pe, ("nq", s // 2))
                    for i in range(TT):
                        a, n = (0, P) if i == 0 else (P, T)
                        mm(oS[:, a:a + n], qh[:, i * P:(i + 1) * P], ksT[:, g, 0:n], start=True, stop=False)
                        mm(oS[:, a + n - P:a + n], identb[:, :], causb[:, :], start=False, stop=True)
                    for i in range(TT):
                        c = slice(384 + i * CMP_S, 384 + (i + 1) * CMP_S)
                        mm(oS[:, c], qh[:, i * P:(i + 1) * P], kct[:, g * CMP_S:(g + 1) * CMP_S], start=True, stop=False)
                        last = mm(oS[:, c], identb[:, :], cmpb[:, i * CMP_S:(i + 1) * CMP_S], start=False, stop=True)
                    last.then_inc(aux_done, 1)
                    for i in range(TT):
                        a, n = (0, P) if i == 0 else (P, T)
                        mm(oW[:, a:a + n], qh[:, i * P:(i + 1) * P], kwT[:, g, 0:n], start=True, stop=False)
                        last = mm(oW[:, a + n - P:a + n], identb[:, :], causb[:, :], start=False, stop=True)
                    last.then_inc(aux_done, 1)
                if 0 <= s - 1 < NSA_H:
                    oS, oW, e = take(("Ts", s - 1)), take(("Tw", s - 1)), (s - 1) % 2
                    pe.wait_ge(*prob_a.next())
                    for o, p, i in ((oS, pS, 0), (oW, pW, 1)):
                        for a in range(3):
                            nc.tensor.transpose(o[:, a * P:(a + 1) * P], p[:, e, a * P:(a + 1) * P], ident)
                        last = nc.tensor.transpose(o[0:CMP_S, 384:512], pC[:, e, i * CMP_S:(i + 1) * CMP_S], ident)
                        last.then_inc(aux_done, 1)
                if s // 2 + 1 < 8:
                    gemm_t((("nq", "ng")[s % 2], s // 2 + 1), XH, XL)
                if 0 <= s - 2 < NSA_H:
                    g = (s - 2) // 4
                    o = take(("On", s - 2))
                    is_free(pe, ("Ts", s - 2))
                    is_free(pe, ("Tw", s - 2))
                    mm(o[:, 0:T], vcm[0:CMP_S, g, :], ptC[0:CMP_S, :], start=True, stop=False)
                    for n, (p, v) in enumerate(((ptS, vs), (ptW, vw))):
                        mm(o[:, 0:T], v[:, 0, g * P:(g + 1) * P], p[:, 0:T], start=False, stop=False)
                        last = mm(o[:, P:T], v[:, 1, g * P:(g + 1) * P], p[:, T:384], start=False, stop=(n == 1))
                    last.then_inc(aux_done, 1)
            o = [take(("no", i)) for i in range(4)]
            pe.wait_ge(*lo_a.next())
            for c in range(8):
                gemm_d(("no", c), o, MH, ML, 2 * c, c == 0, c == 7)
            ple(1)
            assert tiles[0] == NT and uses[0] == len(BANKS)

        @block.scalar
        def _(act):
            n_round, n_sq, chain = [0], [0], [0]
            act_fn = nc.scalar.activation
            rstd_a, max_a, dve_a, x_a = None, After(max_done), After(dve_for_act), None

            def upto(key):
                while n_round[0] < min(TILE[key] + RING, NT):
                    t = n_round[0]
                    n_round[0] += 1
                    act.wait_ge(w_loaded[t % RING], 16 * (t // RING + 1))
                    if t >= RING:
                        act.wait_ge(w_used, t - RING + 1)
                    act_fn(WH[:, t % RING, :], RAW[:, t % RING, :], ACT.Copy).then_inc(w_rounded, 1)

            def link(ins):
                chain[0] += 1
                ins.then_inc(act_chain, 1)

            def sync():
                act.wait_ge(act_chain, chain[0])

            def squares(n, src):
                if n in x_versions and x_versions[n]:
                    act.wait_ge(x_new, x_versions[n])
                for i in range(TT):
                    if n_sq[0]:
                        act.wait_ge(sq_done, n_sq[0])
                    n_sq[0] += 1
                    act_fn(junk[:, :], src[:, i, :], ACT.Square, accum_out=ss[:, n, i:i + 1]).then_inc(sq_done, 1)

            def norm(n, src):
                squares(n, src)
                for j in range(4):
                    ready(act, ("tr", n, j))
                    for kk in range(2):
                        k = 2 * j + kk
                        for v, g in enumerate(norms[n]):
                            act_fn((XH, MH)[v][:, k, :], B(("tr", n, j))[:, kk * T:(kk + 1) * T], ACT.Copy,
                                   scale=col(g, k)).then_inc(hi_done, 1)

            def attention(base, units, blocks_at):
                n = len(units)
                for s in range(n + 3):
                    if s < n:
                        e, kind = s % 2, units[s][0]
                        segs = [(0, T), (T, T)] if kind == "mem" else [(0, P), (P, T)]
                        act.wait_ge(*max_a.next())
                        for i, (a, w) in enumerate(segs):
                            ins = act_fn(prob[:, e, a:a + w], B(("S", base + s))[:, a:a + w], ACT.Exp,
                                         bias=stat[:, 2 * e + i:2 * e + i + 1], scale=DH ** -0.5,
                                         accum_out=stat[:, 4 + 2 * e + i:5 + 2 * e + i])
                            if i == 0:
                                ins.then_inc(exp_done, 1)
                        free(ins, ("S", base + s), "act")
                    if s >= 3 and (s - 3) % 2 == 1:
                        m = s - 4
                        ready(act, ("O", base + m))
                        act_fn(MH[:, blocks_at[m // 2], :], B(("O", base + m))[:, 0:T], ACT.Copy).then_inc(hi_done, 1)

            def ffn(l):
                for s in range(FSTEP):
                    e = s % 2
                    for q, name in enumerate(("fg", "fv")):
                        upto((name, l, s))
                        ready(act, (name, l, s))
                        for b in range(2):
                            f = q * 22 + 2 * s + b
                            act_fn(fy[:, e, (2 * q + b) * T:(2 * q + b + 1) * T], B((name, l, s))[:, b * T:(b + 1) * T],
                                   ACT.Identity, bias=col(f"b_dw_f{l}", f), scale=col(f"w_dw_f{l}", 2 * 44 + f)).then_inc(act_for_dve, 1)
                        if q == 0:
                            act.wait_ge(*dve_a.next())
                            act_fn(fth[:, e, :], fy[:, e, 0:2 * T], ACT.Tanh, scale=0.5).then_inc(act_for_dve, 1)
                    upto(("fd", l, s - 1) if s else ("fv", l, 0))
                    act.wait_ge(*dve_a.next())
                    act_fn(MH[:, 2 * e:2 * e + 2, :], fa[:, e, :].rearrange("p (b t) -> p b t", b=2), ACT.Copy).then_inc(hi_done, 1)

            def ple(l):
                ready(act, ("pt", l))
                act_fn(PH[:, :, :], B(("pt", l))[:, :].rearrange("p (k t) -> p k t", k=2), ACT.Copy).then_inc(hi_done, 1)
                norm(6 + 2 * l, x)
                upto(("pe", l))
                for c in range(4):
                    upto((f"pg{l}", c))
                for i in range(4):
                    ready(act, (f"pg{l}", i))
                    act_fn(pth[:, i, :], B((f"pg{l}", i))[:, :], ACT.Tanh, scale=0.5).then_inc(act_for_dve, 1)

            act.wait_ge(mem_loaded, 16)
            squares(0, memx)
            act.wait_ge(small_loaded, 48)
            act.wait_ge(x_loaded, 16)
            squares(1, x)
            for t in range(RING):
                upto(TILES[0])
            for j in range(4):
                ready(act, ("tr", 0, j))
                for kk in range(2):
                    act_fn(XH[:, 2 * j + kk, :], B(("tr", 0, j))[:, kk * T:(kk + 1) * T], ACT.Copy,
                           scale=col("g_mem", 2 * j + kk)).then_inc(hi_done, 1)
            sw = PCOL["w_f"][0]
            act_fn(SWH[:, :], par[:, sw:sw + KD * (FOX + 48)], ACT.Copy).then_inc(sw_rounded, 1)
            for l in range(2):
                upto(("mk", l))
                ready(act, ("mk", l))
                free(act_fn(mkt[:, l, :, :], B(("mk", l))[:, :].rearrange("p (b t) -> p b t", b=2), ACT.Copy), ("mk", l), "act")
                upto(("mv", l))
                ready(act, ("mv", l))
                free(act_fn(mvv[:, l, :, :], B(("mv", l))[:, :].rearrange("p (b t) -> p b t", b=2), ACT.Copy), ("mv", l), "act")
            for j in range(4):
                ready(act, ("tr", 1, j))
                for kk in range(2):
                    act_fn(XH[:, 2 * j + kk, :], B(("tr", 1, j))[:, kk * T:(kk + 1) * T], ACT.Copy,
                           scale=col("g_mix0", 2 * j + kk)).then_inc(hi_done, 1)
            act.wait_ge(prepared, 1)
            for j in range(3):
                upto(("ca", j))
                ready(act, ("ca", j))
                if j:
                    act.wait_ge(*dve_a.next())
                for b in range(2):
                    ins = act_fn(glu_a[:, b, :], B(("ca", j))[:, b * T:(b + 1) * T], ACT.Identity, scale=0.5,
                                 bias=hbglu[:, 2 * j + b:2 * j + b + 1])
                free(ins, ("ca", j), "act")
                upto(("cg", j))
                ready(act, ("cg", j))
                for b in range(2):
                    ins = act_fn(glu_t[:, b, :], B(("cg", j))[:, b * T:(b + 1) * T], ACT.Tanh, scale=0.5,
                                 bias=hbglu[:, NMB + 2 * j + b:NMB + 2 * j + b + 1])
                free(ins, ("cg", j), "act")
                act.drain().then_inc(act_for_dve, 1)
            upto(("qm", 0))
            ready(act, ("qm", 0))
            link(act_fn(q_mem, B(("qm", 0))[:, :].rearrange("p (b t) -> p b t", b=2), ACT.Copy))
            free(act.drain(), ("qm", 0), "act")
            act.drain().then_inc(act_for_pe, 1)
            attention(0, [("mem", 0, h) for h in range(4)], [NMB, NMB + 1])
            act.wait_ge(*dve_a.next())
            act_fn(lnsq, conv, ACT.Square).then_inc(act_for_pe, 1)
            act.wait_ge(*dve_a.next())
            act_fn(rs_ln, rs_ln, ACT.Sqrt).then_inc(act_for_dve, 1)
            act.wait_ge(*dve_a.next())
            for b in range(NMB):
                link(act_fn(z[:, b, :], conv[:, b, :], ACT.Identity, scale=col("ln_g", b), bias=col("ln_b", b)))
            sync()
            act_fn(lnsq, z, ACT.Tanh, scale=0.5).then_inc(act_for_dve, 1)
            act.wait_ge(*dve_a.next())
            act_fn(MH[:, 0:NMB, :], conv, ACT.Copy, scale=0.5).then_inc(hi_done, 1)
            for c in range(4):
                upto(("o0", c))
            norm(2, x)
            ffn(0)
            for c in range(1):
                upto(("fd", 0, FSTEP - 1))
            norm(3, x)
            for j in range(3):
                upto(("v1", j))
                ready(act, ("v1", j))
                free(act_fn(v1[:, :, j * 256:(j + 1) * 256], B(("v1", j))[:, :].rearrange("p (i f) -> p i f", i=TT), ACT.Copy),
                     ("v1", j), "act")
            for n, dst in (("k1", k1), ("q1", q1)):
                for j in range(3):
                    upto((n, j))
                    ready(act, (n, j))
                    free(act_fn(dst[:, 2 * j:2 * j + 2, :], B((n, j))[:, :].rearrange("p (b t) -> p b t", b=2), ACT.Copy),
                         (n, j), "act")
            upto(("qm", 1))
            ready(act, ("qm", 1))
            link(act_fn(q_mem, B(("qm", 1))[:, :].rearrange("p (b t) -> p b t", b=2), ACT.Copy))
            free(act.drain(), ("qm", 1), "act")
            act.wait_ge(*dve_a.next())
            link(act_fn(lf[:, 1, :], lf[:, 1, :], ACT.Exp))
            sync()
            act_fn(lf[:, 2, :], lf[:, 1, :], ACT.Ln, bias=1.0).then_inc(act_for_dve, 1)
            act.drain().then_inc(act_for_pe, 1)
            attention(4, [("fox", h) for h in range(FOX)] + [("mem", 1, h) for h in range(4)],
                      list(range(NMB)) + [NMB, NMB + 1])
            for c in range(4):
                upto(("o1", c))
            norm(4, x)
            ffn(1)
            upto(("fd", 1, FSTEP - 1))
            squares(9, x)
            norm(5, x)
            for h in range(RH):
                upto(("rq", h))
                upto(("rk", h))

            def ret_out(h):
                for j in range(2):
                    ready(act, ("ry", h, j))
                    for kk in range(2):
                        f = 4 * h + 2 * j + kk
                        act_fn(MH[:, f, :], B(("ry", h, j))[:, kk * T:(kk + 1) * T], ACT.Copy, scale=hgn[:, f:f + 1]).then_inc(hi_done, 1)

            for h in range(RH):
                upto(("rv", h, 1))
                for i in range(TT):
                    ready(act, ("rv", h, i, "out"))
                    free(act_fn(rv[:, i, :], B(("rv", h, i, "out"))[:, :], ACT.Copy), ("rv", h, i, "out"), "act")
                upto(("rg", h, 1))
                for i in range(TT):
                    ready(act, ("rg", h, i, "out"))
                    act_fn(rth[:, i, :], B(("rg", h, i, "out"))[:, :], ACT.Tanh, scale=0.5).then_inc(act_for_dve, 1)
                if h:
                    ret_out(h - 1)
            ret_out(RH - 1)
            for c in range(8):
                upto(("ro", c))
            ple(0)
            norm(7, x)
            for n, dst in (("kc", kvc[:, 0:4, :]), ("vc", kvc[:, 4:8, :]), ("ks", ksT), ("kw", kwT)):
                for j in range(2):
                    upto((n, j))
                    ready(act, (n, j))
                    ins = act_fn(dst[:, 2 * j:2 * j + 2, :], B((n, j))[:, :].rearrange("p (b t) -> p b t", b=2), ACT.Copy)
                    free(ins, (n, j), "act")
            for n, dst in (("vs", vs), ("vw", vw)):
                upto((n, 0))
                upto((n, 1))
                for i in range(TT):
                    ready(act, (n, i, "out"))
                    free(act_fn(dst[:, i, :], B((n, i, "out"))[:, :], ACT.Copy), (n, i, "out"), "act")
            ready(act, ("bg",))
            link(act_fn(g3.rearrange("p i c -> p (i c)"), B(("bg",))[:, 0:TT * 48], ACT.Tanh, scale=0.5))
            free(act.drain(), ("bg",), "act")
            sync()
            act.drain().then_inc(act_for_dve, 1)
            act.wait_ge(*dve_a.next())
            act_fn(MH[:, :, :], blocks.rearrange("p l c -> p (l c)").rearrange("p (a b) -> p a b", a=16), ACT.Copy).then_inc(hi_done, 1)
            for j in range(4):
                upto(("c1k", j))
            for j in range(3):
                upto(("c1v", j))
            for n, r in (("hk", slice(0, 64)), ("hv", slice(64, P))):
                ready(act, (n,))
                if n == "hv":
                    upto(("c1v", 3))
                free(act_fn(hx[r, :], B((n,))[r, 0:256], ACT.Copy), (n,), "act")
            is_free(act, ("hv",))
            act_fn(hs, hx, ACT.Square).then_inc(act_for_dve, 1)
            act.wait_ge(*dve_a.next())
            act_fn(hth, hs, ACT.Tanh, scale=GELU_C).then_inc(act_for_dve, 1)
            ready(act, ("ht",))
            free(act_fn(hT.rearrange("p j c -> p (j c)"), B(("ht",))[:, 0:2 * P], ACT.Copy, scale=0.5), ("ht",), "act")
            ready(act, ("kct",))
            free(act_fn(kct, B(("kct",))[:, 0:64], ACT.Copy), ("kct",), "act")
            ready(act, ("vcm",))
            free(act_fn(vcm[0:CMP_S, :, :].rearrange("p g c -> p (g c)"), B(("vcm",))[0:CMP_S, :], ACT.Copy), ("vcm",), "act")

            def queries(t):
                upto(("nq", t))
                ready(act, ("nq", t))
                free(act_fn(qb[:, t % 2, :], B(("nq", t))[:, :], ACT.Copy), ("nq", t), "act")

            queries(0)
            for s in range(NSA_H + 3):
                if 0 <= s - 2 < NSA_H:
                    o = B(("Tw", s - 2))
                    ready(act, ("Tw", s - 2))
                    if s > 2:
                        ready(act, ("On", s - 3))
                    link(act_fn(ptW, o[:, 0:384], ACT.Copy))
                    free(act_fn(ptC[0:CMP_S, P:T], o[0:CMP_S, 384:512], ACT.Copy), ("Tw", s - 2), "act")
                if s % 2 == 1 and (s + 1) // 2 < 8:
                    queries((s + 1) // 2)
                if s % 2 == 0 and s // 2 < 8:
                    upto(("ng", s // 2))
                    ready(act, ("ng", s // 2))
                    act_fn(nth, B(("ng", s // 2))[:, :], ACT.Tanh, scale=0.5).then_inc(act_for_dve, 1)
                if s < NSA_H:
                    e = s % 2
                    act.wait_ge(*max_a.next())
                    for br, (dst, name) in enumerate(((pC, "Ss"), (pS, "Ss"), (pW, "Sw"))):
                        for i in range(TT):
                            if br == 0:
                                a, b, w = 384 + i * CMP_S, i * CMP_S, CMP_S
                            else:
                                a, b, w = (0, 0, P) if i == 0 else (P, P, T)
                            c = 8 * e + 2 * br + i
                            ins = act_fn(dst[:, e, b:b + w], B((name, s))[:, a:a + w], ACT.Exp, bias=stat[:, c:c + 1],
                                         scale=P ** -0.5, accum_out=stat[:, 16 + c:17 + c])
                        if br == 1:
                            free(ins, ("Ss", s), "act")
                    free(ins, ("Sw", s), "act")
                if 0 <= s - 3 < NSA_H:
                    act.wait_ge(*dve_a.next())
                    act_fn(MH[:, s - 3, :], om[:, (s - 3) % 2, :], ACT.Copy).then_inc(hi_done, 1)
            for c in range(8):
                upto(("no", c))
            ple(1)
            squares(10, x)

        @block.vector
        def _(dve):
            n_split, chain = [0], [0]
            hi_a, act_a, rstd_a = After(hi_done), After(act_for_dve), After(rstd_done)
            exp_a, gn_a, gf_a = None, After(gn_rstd), After(gf_loaded)
            tt, ts, stt, copy = nc.vector.tensor_tensor, nc.vector.tensor_scalar, nc.vector.scalar_tensor_tensor, nc.vector.tensor_copy

            def upto(key):
                while n_split[0] < min(TILE[key] + RING, NT):
                    t = n_split[0]
                    n_split[0] += 1
                    dve.wait_ge(w_rounded, t + 1)
                    tt(WL[:, t % RING, :], RAW[:, t % RING, :], WH[:, t % RING, :].bitcast(F32), ALU.subtract).then_inc(w_split, 1)

            def link(ins):
                chain[0] += 1
                ins.then_inc(dve_chain, 1)

            def sync():
                dve.wait_ge(dve_chain, chain[0])

            def normed(n, src):
                dve.wait_ge(*rstd_a.next())
                for i in range(TT):
                    ts(xn[:, i, :], src[:, i, :], rstd[:, n, i:i + 1], None, ALU.mult).then_inc(xn_done, 1)

            def low_parts(n):
                for j in range(4):
                    dve.wait_ge(*hi_a.next(2 * len(norms[n])))
                    for kk in range(2):
                        k = 2 * j + kk
                        for v, g in enumerate(norms[n]):
                            ins = stt((XL, ML)[v][:, k, :], B(("tr", n, j))[:, kk * T:(kk + 1) * T], col(g, k),
                                      (XH, MH)[v][:, k, :].bitcast(F32), ALU.mult, ALU.subtract)
                    free(ins, ("tr", n, j), "dve")

            def norm(n, src):
                normed(n, src)
                low_parts(n)

            def residual(key):
                for i in range(TT):
                    for half in range(2):
                        c = slice(half * 512, half * 512 + 512)
                        ready(dve, (key, 2 * i + half))
                        free(tt(x[:, i, c], B((key, 2 * i + half))[:, :], x[:, i, c], ALU.add), (key, 2 * i + half), "dve")
                    is_free(dve, (key, 2 * i + 1))
                    dve.drain().then_inc(x_new, 1)

            def attention(base, units, blocks_at):
                n = len(units)
                exp_n = [base]
                for s in range(n + 3):
                    if 0 <= s - 2 < n:
                        w = 512 if units[s - 2][0] == "mem" else 384
                        ready(dve, ("T", base + s - 2))
                        copy(probT[:, (s - 2) % 2, 0:w], B(("T", base + s - 2))[:, 0:w]).then_inc(pt_done, 1)
                        free(dve.drain(), ("T", base + s - 2), "dve")
                    if s < n:
                        e, kind = s % 2, units[s][0]
                        ready(dve, ("S", base + s))
                        o = B(("S", base + s))
                        mx = stat[:, 8 + 2 * e:10 + 2 * e]
                        if kind == "mem":
                            link(nc.vector.tensor_reduce(mx, o[:, :].rearrange("p (i k) -> p i k", i=2), AX_X, ALU.max))
                        else:
                            link(nc.vector.tensor_reduce(mx[:, 0:1], o[:, 0:P], AX_X, ALU.max))
                            link(nc.vector.tensor_reduce(mx[:, 1:2], o[:, P:384], AX_X, ALU.max))
                        sync()
                        ts(stat[:, 2 * e:2 * e + 2], mx, -DH ** -0.5, None, ALU.mult).then_inc(max_done, 1)
                    if 0 <= s - 1 < n:
                        e, kind = (s - 1) % 2, units[s - 1][0]
                        segs = [(0, T), (T, T)] if kind == "mem" else [(0, P), (P, T)]
                        is_free(dve, ("S", base + s - 1))
                        link(nc.vector.reciprocal(stat[:, 12 + 2 * e:14 + 2 * e], stat[:, 4 + 2 * e:6 + 2 * e]))
                        sync()
                        for i, (a, w) in enumerate(segs):
                            ins = ts(prob[:, e, a:a + w], prob[:, e, a:a + w], stat[:, 12 + 2 * e + i:13 + 2 * e + i], None, ALU.mult)
                        ins.then_inc(prob_done, 1)
                    if s >= 3 and (s - 3) % 2 == 1:
                        m = s - 4
                        dve.wait_ge(*hi_a.next())
                        b = blocks_at[m // 2]
                        free(tt(ML[:, b, :], B(("O", base + m))[:, 0:T], MH[:, b, :].bitcast(F32), ALU.subtract),
                             ("O", base + m), "dve")

            def low_signal():
                dve.drain().then_inc(lo_done, 1)

            def ffn(l):
                for s in range(FSTEP):
                    e = s % 2
                    y = fy[:, e, :].rearrange("p (b t) -> p b t", b=4)
                    for q, name in enumerate(("fg", "fv")):
                        upto((name, l, s))
                        dve.wait_ge(*act_a.next(2))
                        for b in range(2):
                            f = q * 22 + 2 * s + b
                            u, yy = B((name, l, s))[:, b * T:(b + 1) * T], y[:, 2 * q + b, :]
                            link(stt(yy[:, 1:T], u[:, 0:T - 1], col(f"w_dw_f{l}", 44 + f), yy[:, 1:T], ALU.mult, ALU.add))
                        sync()
                        for b in range(2):
                            f = q * 22 + 2 * s + b
                            u, yy = B((name, l, s))[:, b * T:(b + 1) * T], y[:, 2 * q + b, :]
                            ins = stt(yy[:, 2:T], u[:, 0:T - 2], col(f"w_dw_f{l}", f), yy[:, 2:T], ALU.mult, ALU.add)
                            if b == 0:
                                link(ins)
                        free(ins, (name, l, s), "dve")
                        is_free(dve, (name, l, s))
                        if q == 0:
                            dve.drain().then_inc(dve_for_act, 1)
                            dve.wait_ge(*act_a.next())
                            link(stt(fth[:, e, :], fth[:, e, :], 1.0, fy[:, e, 0:2 * T], ALU.add, ALU.mult))
                    sync()
                    stt(fa[:, e, :], fth[:, e, :], 0.5, fy[:, e, 2 * T:4 * T], ALU.mult, ALU.mult).then_inc(dve_for_act, 1)
                    upto(("fd", l, s - 1) if s else ("fv", l, 0))
                    dve.wait_ge(*hi_a.next())
                    tt(ML[:, 2 * e:2 * e + 2, :], fa[:, e, :].rearrange("p (b t) -> p b t", b=2),
                       MH[:, 2 * e:2 * e + 2, :].bitcast(F32), ALU.subtract).then_inc(lo_done, 1)
                upto(("fd", l, FSTEP - 1))
                residual(f"f{l}")

            def ple(l):
                ready(dve, ("pt", l))
                dve.wait_ge(*hi_a.next())
                free(tt(PL[:, :, :], B(("pt", l))[:, :].rearrange("p (k t) -> p k t", k=2), PH[:, :, :].bitcast(F32), ALU.subtract),
                     ("pt", l), "dve")
                norm(6 + 2 * l, x)
                for c in range(4):
                    upto((f"pg{l}", c))
                for i in range(4):
                    dve.wait_ge(*act_a.next())
                    ready(dve, ("pe", l, i))
                    free(stt(pth[:, i, :], pth[:, i, :], 1.0, B(("pe", l, i))[:, :], ALU.add, ALU.mult), ("pe", l, i), "dve")
                    is_free(dve, ("pe", l, i))
                    c = slice((i % 2) * 512, (i % 2) * 512 + 512)
                    link(stt(x[:, i // 2, c], pth[:, i, :], 0.5, x[:, i // 2, c], ALU.mult, ALU.add))
                    free(dve.drain(), (f"pg{l}", i), "dve")
                    if i % 2:
                        sync()
                        dve.drain().then_inc(x_new, 1)

            dve.wait_ge(small_loaded, 48)
            link(copy(identb[:, :], ident))
            link(copy(causb[:, :], const("causal")))
            link(copy(cmpb[:, :], const("cmpmask")))
            link(ts(hbglu[:, :], col("b_glu"), 0.5, None, ALU.mult))
            link(ts(hgn[:, :], col("ret_gn"), 0.5, None, ALU.mult))
            sync()
            dve.drain().then_inc(prepared, 1)
            normed(0, memx)
            upto(TILES[0])
            low_parts(0)
            dve.wait_ge(sw_rounded, 1)
            sw = PCOL["w_f"][0]
            tt(SWL[:, :], par[:, sw:sw + KD * (FOX + 48)], SWH[:, :].bitcast(F32), ALU.subtract).then_inc(sw_split, 1)
            for l in range(2):
                upto(("mk", l))
                upto(("mv", l))
            dve.wait_ge(aux_done, USES.ready[("tr", 0, 3)][1])
            norm(1, x)
            link(nc.vector.memset(vpad[:, :, 0:CONV - 1], 0.0))
            for j in range(3):
                upto(("cg", j))
                dve.wait_ge(*act_a.next())
                stt(vpad[:, 2 * j:2 * j + 2, CONV - 1:CONV - 1 + T], glu_t, 1.0, glu_a, ALU.add, ALU.mult).then_inc(dve_for_act if j < 2 else dve_chain, 1)
            chain[0] += 1
            upto(("qm", 0))
            dve.wait_ge(dve_for_act, 2)
            sync()
            w0 = PCOL["w_dw_a"][0]

            def tap(b, k):
                return par[:, w0 + k * NMB + b:w0 + k * NMB + b + 1]

            for b in range(NMB):
                link(ts(conv[:, b, :], vpad[:, b, CONV - 1:CONV - 1 + T], tap(b, CONV - 1), col("b_dw_a", b), ALU.mult, ALU.add))
            sync()
            for k in range(CONV - 1):
                for b in range(NMB):
                    if k:
                        dve.wait_ge(dve_chain, chain[0] - NMB + 1)
                    link(stt(conv[:, b, :], vpad[:, b, k:k + T], tap(b, k), conv[:, b, :], ALU.mult, ALU.add))
            attention(0, [("mem", 0, h) for h in range(4)], [NMB, NMB + 1])
            sync()
            dve.drain().then_inc(dve_for_pe, 1)
            ready(dve, ("mean",))
            tt(conv, conv, B(("mean",))[:, 0:T].unsqueeze(1).to_broadcast([P, NMB, T]), ALU.subtract).then_inc(dve_for_act, 1)
            free(dve.drain(), ("mean",), "dve")
            ready(dve, ("var",))
            ts(rs_ln, B(("var",))[:, 0:T], LN_EPS, None, ALU.add).then_inc(dve_for_act, 1)
            free(dve.drain(), ("var",), "dve")
            dve.wait_ge(*act_a.next())
            link(nc.vector.reciprocal(rs_ln, rs_ln))
            sync()
            tt(conv, conv, rs_ln.unsqueeze(1).to_broadcast([P, NMB, T]), ALU.mult).then_inc(dve_for_act, 1)
            dve.wait_ge(*act_a.next())
            stt(conv, lnsq, 1.0, z, ALU.add, ALU.mult).then_inc(dve_for_act, 1)
            dve.wait_ge(*hi_a.next())
            link(stt(ML[:, 0:NMB, :], conv, 0.5, MH[:, 0:NMB, :].bitcast(F32), ALU.mult, ALU.subtract))
            sync()
            low_signal()
            for c in range(4):
                upto(("o0", c))
            residual("o0")
            norm(2, x)
            ffn(0)
            norm(3, x)
            for n in ("v1", "k1", "q1"):
                for j in range(3):
                    upto((n, j))
            upto(("qm", 1))
            ready(dve, ("fl",))
            zf, az = lf[:, 0, :], lf[:, 1, :]
            free(tt(zf.rearrange("p (i h) -> p i h", i=TT), B(("fl",))[:, 0:TT * FOX].rearrange("p (i h) -> p i h", i=TT),
                    bfree[:, :].unsqueeze(1).to_broadcast([P, TT, FOX]), ALU.add), ("fl",), "dve")
            is_free(dve, ("fl",))
            link(stt(az, zf, -1.0, zf, ALU.mult, ALU.max))
            sync()
            link(ts(az, az, -1.0, None, ALU.mult))
            sync()
            dve.drain().then_inc(dve_for_act, 1)
            dve.wait_ge(*act_a.next())
            stt(lf[:, 3, :], zf, 0.0, lf[:, 2, :], ALU.min, ALU.subtract).then_inc(dve_for_pe, 1)
            ready(dve, ("cum",))
            link(copy(cumT[0:FOX, 0, :], B(("cum",))[0:FOX, 0:T]))
            free(ts(cumT[0:FOX, 1, :], B(("cum",))[0:FOX, 0:T], -1.0, None, ALU.mult), ("cum",), "dve")
            dve.drain().then_inc(dve_for_pe, 1)
            attention(4, [("fox", h) for h in range(FOX)] + [("mem", 1, h) for h in range(4)],
                      list(range(NMB)) + [NMB, NMB + 1])
            is_free(dve, ("O", 18))
            low_signal()
            for c in range(4):
                upto(("o1", c))
            residual("o1")
            norm(4, x)
            ffn(1)
            dve.wait_ge(*rstd_a.next())
            dve.wait_ge(*gf_a.next(16))
            for i in range(TT):
                dve.wait_ge(x_new, 8)
                stt(x[:, i, :], x[:, i, :], rstd[:, 9, i:i + 1], gfree[:, :], ALU.mult, ALU.mult).then_inc(x_new, 1)
            dve.wait_ge(x_new, 10)
            norm(5, x)
            for h in range(RH):
                for name, dst in (("rq", qr), ("rk", kr)):
                    upto((name, h))
                    ready(dve, (name, h))
                    o = B((name, h))
                    sync()
                    link(tt(rm[:, 0, :], o[:, :], const("cossin"), ALU.mult))
                    ins = tt(rm[:, 1, :], o[:, :], const("sincos"), ALU.mult)
                    free(ins, (name, h), "dve")
                    is_free(dve, (name, h))
                    sync()
                    link(tt(dst[:, h, 0:T], rm[:, 0, 0:T], rm[:, 0, T:2 * T], ALU.subtract))
                    link(tt(dst[:, h, T:2 * T], rm[:, 1, 0:T], rm[:, 1, T:2 * T], ALU.add))
            dve.drain().then_inc(dve_for_pe, 1)

            def ret_low(h):
                for j in range(2):
                    dve.wait_ge(*hi_a.next(2))
                    for kk in range(2):
                        f = 4 * h + 2 * j + kk
                        ins = stt(ML[:, f, :], B(("ry", h, j))[:, kk * T:(kk + 1) * T], hgn[:, f:f + 1],
                                  MH[:, f, :].bitcast(F32), ALU.mult, ALU.subtract)
                    free(ins, ("ry", h, j), "dve")

            for h in range(RH):
                upto(("rv", h, 1))
                upto(("rg", h, 1))
                for i in range(TT):
                    dve.wait_ge(*act_a.next())
                    ins = stt(rgs[:, i, :], rth[:, i, :], 1.0, B(("rg", h, i, "out"))[:, :], ALU.add, ALU.mult)
                    free(ins, ("rg", h, i, "out"), "dve")
                ready(dve, ("rs", h))
                free(tt(sdt[:, h % 2, :], B(("rs", h))[:, 0:384], const("decay")[:, h * 384:(h + 1) * 384], ALU.mult), ("rs", h), "dve")
                a = 16 + 4 * (h % 2)
                for i in range(TT):
                    ready(dve, ("ro", h, i))
                    link(nc.vector.bn_stats(stat[:, 32 + 6 * i:38 + 6 * i], B(("ro", h, i))[:, :]))
                sync()
                for i in range(TT):
                    link(nc.vector.bn_aggr(stat[:, 24 + 2 * i:26 + 2 * i], stat[:, 32 + 6 * i:38 + 6 * i]))
                sync()
                for i in range(TT):
                    link(ts(stat[:, a + i:a + i + 1], stat[:, 25 + 2 * i:26 + 2 * i], RMS_EPS, None, ALU.add))
                sync()
                dve.drain().then_inc(gn_stat, 1)
                if h:
                    ret_low(h - 1)
                dve.wait_ge(*gn_a.next())
                is_free(dve, ("rg", h, 1, "out"))
                for i in range(TT):
                    free(ts(ry[:, i, :], B(("ro", h, i))[:, :], stat[:, 24 + 2 * i:25 + 2 * i], stat[:, a + 2 + i:a + 3 + i],
                            ALU.subtract, ALU.mult), ("ro", h, i), "dve")
                is_free(dve, ("ro", h, 1))
                for i in range(TT):
                    link(tt(ry[:, i, :], ry[:, i, :], rgs[:, i, :], ALU.mult))
                dve.drain().then_inc(dve_for_pe, 1)
            ret_low(RH - 1)
            for c in range(8):
                upto(("ro", c))
            residual("ro")
            ple(0)
            norm(7, x)
            for n in ("kc", "vc", "ks", "kw", "vs", "vw"):
                for j in range(2):
                    upto((n, j))
            is_free(dve, ("vc", 1))
            link(nc.vector.memset(blocks[:, CMP_S:CMP_L, CMP_S - 1:P:CMP_S], 0.0))
            for v, pe_name in enumerate(("pe_k", "pe_v")):
                src = kvc[:, 4 * v:4 * v + 4, :].rearrange("p g (n l) -> p g l n", l=CMP_S)
                pos = col(pe_name)
                for half in range(2):
                    n = CMP_S - half
                    dst = blocks[:, half * CMP_S:(half + 1) * CMP_S, v * 64:(v + 1) * 64].rearrange("p l (g n) -> p g l n", g=4)
                    for g in range(4):
                        link(tt(dst[:, g, :, 0:n], src[:, g, :, half:CMP_S],
                                pos[:, half * CMP_S:(half + 1) * CMP_S].unsqueeze(2).to_broadcast([P, CMP_S, n]), ALU.add))
            sync()
            dve.wait_ge(*act_a.next())
            link(ts(g3.rearrange("p i c -> p (i c)"), g3.rearrange("p i c -> p (i c)"), 0.5, 0.5, ALU.mult, ALU.add))
            sync()
            for i in range(TT):
                gv = g3[:, i, :].rearrange("p (h b) -> p h b", b=3)[:, :, 0]
                link(ts(gv, gv, const("rowvalid")[:, i:i + 1], None, ALU.mult))
            sync()
            is_free(dve, ("vw", 1, "out"))
            dve.drain().then_inc(dve_for_act, 1)
            dve.wait_ge(*hi_a.next())
            link(tt(ML[:, :, :], blocks.rearrange("p l c -> p (l c)").rearrange("p (a b) -> p a b", a=16),
                    MH[:, :, :].bitcast(F32), ALU.subtract))
            sync()
            low_signal()
            for j in range(4):
                upto(("c1k", j))
            for j in range(4):
                upto(("c1v", j))
            dve.wait_ge(*act_a.next())
            link(ts(hs, hs, 0.044715, 1.0, ALU.mult, ALU.add))
            sync()
            tt(hs, hs, hx, ALU.mult).then_inc(dve_for_act, 1)
            dve.wait_ge(*act_a.next())
            stt(hs, hth, 1.0, hx, ALU.add, ALU.mult).then_inc(dve_for_pe, 1)
            for s in range(NSA_H + 4):
                if s % 2 == 1 and (s + 1) // 2 < 8:
                    upto(("nq", (s + 1) // 2))
                if 0 <= s - 2 < NSA_H:
                    o = B(("Ts", s - 2))
                    ready(dve, ("Ts", s - 2))
                    if s > 2:
                        ready(dve, ("On", s - 3))
                    link(copy(ptS, o[:, 0:384]))
                    free(copy(ptC[0:CMP_S, 0:P], o[0:CMP_S, 384:512]), ("Ts", s - 2), "dve")
                if 0 <= s - 4 < NSA_H:
                    e = (s - 4) % 2
                    dve.wait_ge(*hi_a.next())
                    link(tt(ML[:, s - 4, :], om[:, e, :], MH[:, s - 4, :].bitcast(F32), ALU.subtract))
                if s < NSA_H:
                    e = s % 2
                    oS, oW = B(("Ss", s)), B(("Sw", s))
                    mx = stat[:, 64 + 6 * e:70 + 6 * e]
                    ready(dve, ("Sw", s))
                    link(nc.vector.tensor_reduce(mx[:, 0:2], oS[:, 384:416].rearrange("p (i c) -> p i c", i=2), AX_X, ALU.max))
                    for br, o in ((1, oS), (2, oW)):
                        link(nc.vector.tensor_reduce(mx[:, 2 * br:2 * br + 1], o[:, 0:P], AX_X, ALU.max))
                        link(nc.vector.tensor_reduce(mx[:, 2 * br + 1:2 * br + 2], o[:, P:384], AX_X, ALU.max))
                    sync()
                    ts(stat[:, 8 * e:8 * e + 6], mx, -P ** -0.5, None, ALU.mult).then_inc(max_done, 1)
                if 0 <= s - 1 < NSA_H:
                    e = (s - 1) % 2
                    is_free(dve, ("Sw", s - 1))
                    rc, fac = stat[:, 32 + 12 * e:38 + 12 * e], stat[:, 38 + 12 * e:44 + 12 * e]
                    link(nc.vector.reciprocal(rc, stat[:, 16 + 8 * e:22 + 8 * e]))
                    sync()
                    gh = g3.rearrange("p i (h b) -> p h b i", b=3)[:, s - 1, :, :]
                    link(tt(fac.rearrange("p (b i) -> p b i", b=3), rc.rearrange("p (b i) -> p b i", b=3), gh, ALU.mult))
                    sync()
                    for br, p in enumerate((pC, pS, pW)):
                        for i in range(TT):
                            if br == 0:
                                a, w = i * CMP_S, CMP_S
                            else:
                                a, w = (0, P) if i == 0 else (P, T)
                            ins = ts(p[:, e, a:a + w], p[:, e, a:a + w], fac[:, 2 * br + i:2 * br + i + 1], None, ALU.mult)
                    ins.then_inc(prob_done, 1)
                if 0 <= s - 3 < NSA_H:
                    h = s - 3
                    ready(dve, ("On", h))
                    free(stt(om[:, h % 2, :], B(("On", h))[:, 0:T], 0.5, gs[:, (h // 2) % 2, (h % 2) * T:(h % 2) * T + T],
                             ALU.mult, ALU.mult), ("On", h), "dve")
                    is_free(dve, ("On", h))
                    dve.drain().then_inc(dve_for_act, 1)
                if s % 2 == 0 and s // 2 < 8:
                    upto(("ng", s // 2))
                    dve.wait_ge(*act_a.next())
                    free(stt(gs[:, (s // 2) % 2, :], nth, 1.0, B(("ng", s // 2))[:, :], ALU.add, ALU.mult), ("ng", s // 2), "dve")
                    is_free(dve, ("ng", s // 2))
            sync()
            low_signal()
            for c in range(8):
                upto(("no", c))
            residual("no")
            ple(1)
            dve.wait_ge(*rstd_a.next())
            dve.wait_ge(*gf_a.next(16))
            for i in range(TT):
                stt(xn[:, i, :], x[:, i, :], rstd[:, 10, i:i + 1], gfree[:, :], ALU.mult, ALU.mult).then_inc(out_done, 1)


def tile_of(w, kind, c0, k0=0):
    kb, cols = {"T": (8, 256), "N": (4, 512), "D": (2, 1024)}[kind]
    return w[k0:k0 + kb * P, c0:c0 + cols].reshape(kb, P, cols).transpose(1, 0, 2).reshape(P, kb * cols)


def weight_stream(a):
    def one(key):
        n = key[0]
        if n == "mk":
            return tile_of(a["w_mem_kv"][key[1]], "T", 0)
        if n == "mv":
            return tile_of(a["w_mem_kv"][key[1]], "T", 256)
        if n == "ca":
            return tile_of(a["w_in_a"][0], "T", 256 * key[1])
        if n == "cg":
            return tile_of(a["w_in_a"][0], "T", MIX + 256 * key[1])
        if n == "qm":
            return tile_of(a["w_in_a"][0], "T", 2 * MIX) if key[1] == 0 else tile_of(a["w_in_b"][0], "T", MIX)
        if n in ("o0", "o1"):
            return tile_of(a["w_out"][int(n[1])], "D", 0, 256 * key[1])
        if n == "fg":
            return tile_of(a["w_up"][key[1]], "T", 256 * key[2])
        if n == "fv":
            return tile_of(a["w_up"][key[1]], "T", DFF + 256 * key[2])
        if n == "fd":
            return tile_of(a["w_down"][key[1]], "D", 0, 256 * key[2])
        if n == "k1":
            return tile_of(a["w_kvf"], "T", 256 * key[1])
        if n == "v1":
            return tile_of(a["w_kvf"], "T", MIX + 256 * key[1])
        if n == "q1":
            return tile_of(a["w_in_b"][0], "T", 256 * key[1])
        if n == "rq":
            return tile_of(a["ret_w_in_2"][0], "T", 256 * key[1])
        if n == "rk":
            return tile_of(a["ret_w_in_2"][0], "T", 1024 + 256 * key[1])
        if n == "rv":
            return tile_of(a["ret_w_in_2"][0], "N", 2048 + 512 * key[1], 512 * key[2])
        if n == "rg":
            return tile_of(a["ret_w_in_2"][0], "N", 4096 + 512 * key[1], 512 * key[2])
        if n == "ro":
            return tile_of(a["ret_w_out_2"][0], "D", 0, 256 * key[1])
        if n == "pe":
            return tile_of(a["ple_w_emb_2"][key[1]], "D", 0)
        if n in ("pg0", "pg1"):
            return tile_of(a["ple_w_gate_2"][int(n[2])], "D", 0, 256 * key[1])
        if n in ("kc", "vc", "ks", "kw"):
            c = {"kc": 0, "vc": 512, "ks": 1024, "kw": 2048}[n]
            return tile_of(a["kv_w_2"], "T", c + 256 * key[1])
        if n in ("vs", "vw"):
            return tile_of(a["kv_w_2"], "N", {"vs": 1536, "vw": 2560}[n], 512 * key[1])
        if n in ("c1k", "c1v"):
            w = a["cmp_w1_k_2"] if n == "c1k" else a["cmp_w1_v_2"]
            return tile_of(w, "T", 0, 1024 * key[1])
        if n == "nq":
            return tile_of(a["nsa_w_in_2"][0], "T", 256 * key[1])
        if n == "ng":
            return tile_of(a["nsa_w_in_2"][0], "T", 2048 + 256 * key[1])
        return tile_of(a["nsa_w_out_2"][0], "D", 0, 256 * key[1])

    return np.stack([one(key) for key in TILES])


def param_array(a):
    def cols(v):
        return v.reshape(-1, P).T

    def wide(w):
        return w.reshape(-1, P, w.shape[1]).transpose(1, 0, 2).reshape(P, -1)

    v = {"g_mem": cols(a["g_mem"]), "g_kv": cols(a["g_kv"]), "ret_norm": cols(a["ret_norm_2"][0]),
         "kv_norm": cols(a["kv_norm_2"]), "nsa_norm": cols(a["nsa_norm_2"][0]), "b_glu": cols(a["b_glu"][0]),
         "b_dw_a": cols(a["b_dw_a"][0]), "ln_g": cols(a["ln_g"][0]), "ln_b": cols(a["ln_b"][0]),
         "w_dw_a": cols(a["w_dw_a"][0]), "ret_gn": cols(a["ret_gn_2"][0]), "pe_k": a["cmp_pe_k_2"].T,
         "pe_v": a["cmp_pe_v_2"].T, "w2_k": wide(a["cmp_w2_k_2"]), "w2_v": wide(a["cmp_w2_v_2"]),
         "w_f": wide(a["w_kvf"][:, 2 * MIX:]), "w_bg": wide(a["nsa_w_in_2"][0][:, 4096:])}
    for l in range(2):
        v[f"g_mix{l}"] = cols(a["g_mix"][l])
        v[f"g_ffn{l}"] = cols(a["g_ffn"][l])
        v[f"ple_norm{l}"] = cols(a["ple_norm_2"][l])
        v[f"w_dw_f{l}"] = cols(a["w_dw_f"][l])
        v[f"b_dw_f{l}"] = cols(a["b_dw_f"][l])
    return np.ascontiguousarray(np.concatenate([v[n] for n, _ in PARAM_PARTS], axis=1))


def const_array():
    f8 = np.float64
    half = 128
    inv = (np.float32(10000.0) ** (-np.arange(half, dtype=np.float32) / np.float32(half))).astype(np.float32)
    ang = (np.arange(T, dtype=np.float32)[None, :] * inv[:, None]).astype(f8)
    cos, sin = np.cos(ang), np.sin(ang)
    lg = np.log1p(-(2.0 ** (-5.0 - np.arange(RH, dtype=f8))))
    m, n = np.arange(P)[:, None], np.arange(P)[None, :]
    scale = 256.0 ** -0.5
    decay = []
    for h in range(RH):
        same = np.where(n >= m, np.exp(np.maximum(n - m, 0) * lg[h]), 0.0) * scale
        cross = np.exp((n + 1.0) * lg[h]) * np.exp((P - 1.0 - m) * lg[h]) * scale
        decay.append(np.concatenate([same, cross, same], axis=1))
    t = np.arange(T)
    tri = [8.0 * (np.arange(i * P, (i + 1) * P)[:, None] <= t[None, :]) for i in range(TT)]
    causal = np.where(n <= m, 0.0, NEG)
    cmpm = [np.where(((np.arange(CMP_S)[None, :] * CMP_S + CMP_L - 1 <= np.arange(i * P, (i + 1) * P)[:, None])
                      & (np.arange(CMP_S)[None, :] < CMP_S - 1))
                     | (np.arange(i * P, (i + 1) * P)[:, None] < CMP_L - 1), 0.0, NEG) for i in range(TT)]
    rowv = [(np.arange(i * P, (i + 1) * P)[:, None] >= CMP_L - 1) * 1.0 for i in range(TT)]
    v = {"ident": np.eye(P), "cossin": np.concatenate([cos, sin], 1), "sincos": np.concatenate([sin, cos], 1),
         "decay": np.concatenate(decay, 1), "tri8": np.concatenate(tri, 1), "causal": causal,
         "cmpmask": np.concatenate(cmpm, 1), "rowvalid": np.concatenate(rowv, 1), "ones": np.full((P, P), 1.0 / MIX)}
    return np.ascontiguousarray(np.concatenate([v[n] for n, _ in CONST_PARTS], axis=1).astype(np.float32))


def kernel(**inputs):
    import concourse.bacc as bacc
    from concourse.bass_utils import run_bass_kernel_spmd

    a = {k: np.ascontiguousarray(v) for k, v in inputs.items()}
    arrays = {"wstream": weight_stream(a), "params": param_array(a), "consts": const_array(), "x_in": a["x"],
              "mem_in": a["mem"], "p_in": a["p_2"], "b_f": a["b_f"], "g_final": a["g_final"],
              "final_norm": a["final_norm_2"]}
    nc = bacc.Bacc("TRN2", target_bir_lowering=False, num_devices=1, dynamic_dma_scratch_size=1024)
    args = {n: nc.dram_tensor(n, v.shape, F32, kind="ExternalInput").ap() for n, v in arrays.items()}
    out = nc.dram_tensor("out_dram", (1, T, D), F32, kind="ExternalOutput").ap()
    program(nc, args["wstream"], args["params"], args["consts"], args["x_in"], args["mem_in"], args["p_in"], args["b_f"],
            args["g_final"], args["final_norm"], out)
    r = run_bass_kernel_spmd(nc, [arrays], core_ids=[0])
    return r.results[0]["out_dram"]
```

```python
from contextlib import ExitStack

import numpy as np

import concourse.bass as bass
from concourse import mybir

F32 = mybir.dt.float32
F32R = mybir.dt.float32r
BF16 = mybir.dt.bfloat16
ALU = mybir.AluOpType
ACT = mybir.ActivationFunctionType
AX_X = mybir.AxisListType.X

P = 128
T = 256
TT = T // P
D = 1024
KD = D // P
DH = 64
MIX = 768
NMB = MIX // P
FOX = MIX // DH
CONV = 31
DFF = 2816
FSTEP = DFF // 256
RH = 4
NSA_H = 16
NSA_G = 4
CMP_L = 32
CMP_S = 16
NEG = -1e30
RING = 3
TILE_COLS = 2048
RMS_EPS = 1e-6
LN_EPS = 1e-5
GELU_C = 0.7978845608028654


def layout(parts):
    at, out = 0, {}
    for name, n in parts:
        out[name] = (at, at + n)
        at += n
    return out, at


PARAM_PARTS = [("g_mem", KD), ("g_mix0", KD), ("g_mix1", KD), ("g_ffn0", KD), ("g_ffn1", KD), ("g_kv", KD),
               ("ret_norm", KD), ("ple_norm0", KD), ("ple_norm1", KD), ("kv_norm", KD), ("nsa_norm", KD),
               ("b_glu", 2 * NMB), ("b_dw_a", NMB), ("ln_g", NMB), ("ln_b", NMB), ("w_dw_a", NMB * CONV),
               ("w_dw_f0", 44 * 3), ("w_dw_f1", 44 * 3), ("b_dw_f0", 44), ("b_dw_f1", 44), ("ret_gn", 16),
               ("pe_k", CMP_L), ("pe_v", CMP_L), ("w2_k", 2 * P), ("w2_v", 2 * P),
               ("w_f", KD * FOX), ("w_bg", KD * 48)]
PCOL, N_PARAM = layout(PARAM_PARTS)
CONST_PARTS = [("cossin", 2 * T), ("sincos", 2 * T), ("decay", RH * 384), ("tri8", TT * T),
               ("causal", P), ("cmpmask", TT * CMP_S), ("rowvalid", TT), ("ones", P)]
CCOL, N_CONST = layout(CONST_PARTS)


def plan_tiles():
    t = []
    for j in range(3):
        t += [("ca", j), ("cg", j)]
    t += [("qm", 0)]
    for l in range(2):
        t += [("mk", l), ("mv", l)]
    t += [("o0", c) for c in range(4)]

    def ffn(l):
        out = [("fg", l, 0), ("fv", l, 0)]
        for s in range(1, FSTEP):
            out += [("fg", l, s), ("fv", l, s), ("fd", l, s - 1)]
        return out + [("fd", l, FSTEP - 1)]

    t += ffn(0)
    t += [("v1", j) for j in range(3)]
    for j in range(3):
        t += [("k1", j), ("q1", j)]
    t += [("qm", 1)] + [("o1", c) for c in range(4)]
    t += ffn(1)
    for h in range(RH):
        t += [("rq", h), ("rk", h)]
    for h in range(RH):
        t += [("rv", h, 0), ("rv", h, 1), ("rg", h, 0), ("rg", h, 1)]
    t += [("ro", c) for c in range(8)]
    t += [("pe", 0)] + [("pg0", c) for c in range(4)]
    for n in ("kc", "vc", "ks", "kw"):
        t += [(n, j) for j in range(2)]
    for n in ("vs", "vw"):
        t += [(n, j) for j in range(2)]
    t += [(n, j) for n in ("c1k", "c1v") for j in CMP_ORDER]
    for j in range(8):
        t += [("nq", j), ("ng", j)]
    t += [("no", c) for c in range(8)]
    t += [("pe", 1)] + [("pg1", c) for c in range(4)]
    return t


CMP_ORDER = (2, 3, 0, 1)

TILES = plan_tiles()
TILE = {key: n for n, key in enumerate(TILES)}


PE_CONV = (4, 5)
FOX_TILES = {0: ("k1", 1), 2: ("q1", 1), 4: ("k1", 2), 6: ("q1", 2), 8: ("qm", 1)}


def plan_banks():
    u = []

    def gemm(key, freer, last=None):
        u.append(("A", key, freer, last or key))

    def aux(ring, key, freer):
        u.append((ring, key, freer, None))

    def norm(n):
        for j in range(4):
            aux("A", ("tr", n, j), "dve")

    def acc(key, last):
        for i in range(4):
            u.append(("B", (key, i), "dve", "later" if i < TT else last))
        u.append(("complete", [(key, i) for i in range(TT)], None, None))

    def attention(base, n, between={}):
        for s in range(n + 2):
            if s < n:
                aux("B", ("S", base + s), "act")
            if 0 <= s - 1 < n:
                aux("B", ("T", base + s - 1), "dve")
            if s in between:
                gemm(between[s], "act")
            if 0 <= s - 2 < n:
                if (s - 2) % 2 == 0:
                    u.append(("B", ("O", base + s - 2), "dve_values", "later"))
                else:
                    u.append(("complete", [("O", base + s - 3)], None, None))

    def ffn(l):
        acc(f"f{l}", ("fd", l, FSTEP - 1))
        for s in range(FSTEP):
            gemm(("fg", l, s), "dve")
            gemm(("fv", l, s), "dve")

    norm(1)
    for j in range(3):
        gemm(("ca", j), "act")
        gemm(("cg", j), "act")
    gemm(("qm", 0), "act")
    norm(0)
    for l in range(2):
        gemm(("mk", l), "act")
        gemm(("mv", l), "act")
    for b in PE_CONV:
        aux("B", ("cv", b), "dve")
    attention(0, 4)
    aux("B", ("mean",), "dve")
    aux("B", ("var",), "dve")
    acc("o0", ("o0", 3))
    norm(2)
    ffn(0)
    norm(3)
    for j in range(3):
        gemm(("v1", j), "act")
    aux("A", ("fl",), "dve")
    gemm(("k1", 0), "act")
    aux("A", ("cum",), "dve")
    gemm(("q1", 0), "act")
    attention(4, 16, FOX_TILES)
    acc("o1", ("o1", 3))
    norm(4)
    ffn(1)
    norm(5)
    for h in range(RH):
        gemm(("rq", h), "dve")
        gemm(("rk", h), "dve")
    for h in range(RH):
        for i in range(TT):
            gemm(("rv", h, i, "out"), "act", ("rv", h, 1))
        for i in range(TT):
            gemm(("rg", h, i, "out"), "dve", ("rg", h, 1))
        aux("B", ("rs", h), "dve")
        for i in range(TT):
            aux("B", ("ro", h, i), "dve")
        if h:
            for j in range(2):
                aux("A", ("ry", h - 1, j), "dve")
    for j in range(2):
        aux("A", ("ry", RH - 1, j), "dve")
    acc("ro", ("ro", 7))
    ple(u, norm, acc, 0, 6)
    norm(7)
    for n in ("kc", "vc", "ks", "kw"):
        for j in range(2):
            gemm((n, j), "act")
    for n in ("vs", "vw"):
        for i in range(TT):
            gemm((n, i, "out"), "act", (n, 1))
    aux("A", ("bg",), "act")
    u.append(("B", ("hk",), "act", ("c1k", CMP_ORDER[-1])))
    u.append(("B", ("hv",), "act", ("c1v", CMP_ORDER[-1])))
    gemm(("nq", 0), "act")
    gemm(("ng", 0), "dve")
    aux("B", ("ht",), "act")
    aux("B", ("kct",), "act")
    aux("B", ("vcm",), "act")
    for s in range(NSA_H + 1):
        if s < NSA_H:
            aux("B", ("Ss", s), "act")
            aux("B", ("Sw", s), "act")
        if 0 <= s - 1 < NSA_H:
            aux("A", ("Ts", s - 1), "dve")
            aux("A", ("Tw", s - 1), "act")
        if s // 2 + 1 < 8:
            if s % 2 == 0:
                gemm(("nq", s // 2 + 1), "act")
            else:
                gemm(("ng", s // 2 + 1), "dve")
        if 0 <= s - 1 < NSA_H:
            aux("B", ("On", s - 1), "dve")
    acc("no", ("no", 7))
    ple(u, norm, acc, 1, 8)
    return u


def ple(u, norm, acc, l, n):
    u.append(("A", ("pt", l), "dve", None))
    norm(n)
    for i in range(4):
        u.append(("A", ("pe", l, i), "dve", ("pe", l)))
    acc(f"pg{l}", (f"pg{l}", 3))


BANKS = plan_banks()


class Uses:

    def __init__(self):
        at = {"A": 0, "B": 0}
        freed = {}
        history = {"A": [], "B": []}
        aux = 0
        self.bank, self.ready, self.freed, self.before = {}, {}, {}, {}
        for ring, key, freer, last in BANKS:
            if ring == "complete":
                aux += 1
                for k in key:
                    self.ready[k] = ("aux", aux)
                continue
            assert key not in self.bank, key
            n = at[ring]
            at[ring] += 1
            self.bank[key] = (4 if ring == "A" else 0) + n % 4
            who = (ring, freer)
            freed[who] = freed.get(who, 0) + 1
            self.freed[key] = (who, freed[who])
            self.before[key] = self.freed[history[ring][-4]] if n >= 4 else None
            history[ring].append(key)
            if last is None:
                aux += 1
                self.ready[key] = ("aux", aux)
            elif last != "later":
                self.ready[key] = ("tile", TILE[last] + 1)


USES = Uses()


class After:

    def __init__(self, sem):
        self.sem, self.n = sem, 0

    def next(self, k=1):
        self.n += k
        return self.sem, self.n


def program(nc, wstream, params, consts, ident_in, x_in, mem_in, p_in, b_f, g_final, final_norm, out):
    NT = len(TILES)
    with ExitStack() as ctx:
        def sb(name, shape, dt=F32):
            return ctx.enter_context(nc.sbuf_tensor(name, shape, dt))

        def sem(name):
            return ctx.enter_context(nc.semaphore(name))

        RAW = sb("RAW", [P, RING, TILE_COLS])
        WH = sb("WH", [P, RING, TILE_COLS], F32R)
        WL = sb("WL", [P, RING, TILE_COLS], F32R)
        XH = sb("XH", [P, KD, T], F32R)
        XL = sb("XL", [P, KD, T], F32R)
        MH = sb("MH", [P, 16, T], F32R)
        ML = sb("ML", [P, 16, T], F32R)
        KH, KL = MH[:, 8:16, :], ML[:, 8:16, :]
        SWH = sb("SWH", [P, KD * (FOX + 48)], F32R)
        SWL = sb("SWL", [P, KD * (FOX + 48)], F32R)
        PH = sb("PH", [P, 2, T], F32R)
        PL = sb("PL", [P, 2, T], F32R)
        x = sb("x", [P, TT, D])
        xn = sb("xn", [P, TT, D])
        par = sb("par", [P, N_PARAM])
        con = sb("con", [P, N_CONST])
        ident_sb = sb("ident", [P, P])
        ident = ident_sb[:, :]
        gfree = sb("gfree", [P, D])
        bfree = sb("bfree", [P, FOX])
        junk = sb("junk", [P, D], BF16)
        mkt = sb("mkt", [P, 2, 2, T])
        mvv = sb("mvv", [P, 2, TT, T])
        identb = sb("identb", [P, P], BF16)
        causb = sb("causb", [P, P], BF16)
        cmpb = sb("cmpb", [P, TT * CMP_S], BF16)
        hbglu = sb("hbglu", [P, 2 * NMB])
        hgn = sb("hgn", [P, 16])
        eps = sb("eps", [P, 2])
        mhalf = sb("mhalf", [P, 2])
        ss = sb("ss", [P, 11, 2 * TT])
        ms = sb("ms", [P, 11, TT])
        rstd = sb("rstd", [P, 11, TT])
        stat = sb("stat", [P, 80])
        WORK = 10912
        work = sb("work", [P, WORK])
        bank = [ctx.enter_context(nc.psum_tensor(f"bank{i}", [P, 512], F32)) for i in range(8)]

        def col(name, i=None, n=1):
            a, b = PCOL[name]
            return par[:, a:b] if i is None else par[:, a + i:a + i + n]

        def const(name):
            a, b = CCOL[name]
            return con[:, a:b]

        ones = const("ones")

        def wk(at, *shape):
            n = int(np.prod(shape))
            assert at + n <= WORK, (at, n)
            v = work[:, at:at + n]
            if len(shape) == 2:
                v = v.rearrange("p (a b) -> p a b", a=shape[0])
            if len(shape) == 3:
                v = v.rearrange("p (a b c) -> p a b c", a=shape[0], b=shape[1])
            return v

        memx = wk(3840, TT, D)
        q_mem = wk(0, 2, T)
        q1 = wk(512, NMB, T)
        k1 = wk(2048, NMB, T)
        v1 = wk(3584, TT, MIX)
        prob = wk(5120, 2, 512)
        probT = wk(6144, 2, 512)
        cumT = wk(7168, 2, T)
        lf = wk(7680, 4, TT * FOX)
        vpad = wk(512, NMB, CONV - 1 + T)
        conv = wk(2304, NMB, T)
        lnsq = wk(3840, NMB, T)
        rs_ln = wk(7168, T)
        glu_a = wk(7424, 2, T)
        glu_t = wk(7936, 2, T)
        z = wk(8448, NMB, T)
        DIAGS = 8
        diag = wk(8448, DIAGS, P)
        fy = wk(0, 2, 4 * T)
        fth = wk(2048, 2, 2 * T)
        fa = wk(3072, 2, 2 * T)
        qr = wk(0, RH, 2 * T)
        kr = wk(2048, RH, 2 * T)
        rm = wk(4096, 2, 2 * T)
        sdt = wk(5120, 2, 384)
        rv = wk(5888, TT, 512)
        rth = wk(6912, TT, 512)
        rgs = wk(7936, TT, 512)
        ry = wk(8960, TT, 512)
        pin = wk(10400, TT, T)
        pth = wk(512, 4, 512)
        ksT = wk(0, NSA_G, T)
        kwT = wk(1024, NSA_G, T)
        vs = wk(2048, TT, 512)
        vw = wk(3072, TT, 512)
        kct = wk(4096, 64)
        vcm = wk(4160, NSA_G, P)
        g3 = wk(4672, TT, 48)
        kvc = wk(4768, 8, T)
        blocks = wk(6816, CMP_L, P)
        hx, hs, hth = (xn[:, 1, n * T:(n + 1) * T] for n in range(3))
        hT = xn[:, 1, 3 * T:4 * T].rearrange("p (j c) -> p j c", j=2)
        qb = wk(4768, 2, 2 * T)
        nth = wk(5792, 2 * T)
        gs = wk(6304, 2, 2 * T)
        pS = wk(7328, 2, 384)
        pW = wk(8096, 2, 384)
        pC = wk(8864, 2, TT * CMP_S)
        ptS = wk(8928, 384)
        ptW = wk(9312, 384)
        ptC = wk(9696, T)
        om = xn[:, 0, 0:2 * T].rearrange("p (e t) -> p e t", e=2)

        w_loaded = [sem(f"w_loaded{i}") for i in range(RING)]
        w_rounded = sem("w_rounded")
        w_split = sem("w_split")
        w_used = sem("w_used")
        aux_done = sem("aux_done")
        freed = {(r, e): sem(f"freed_{r}_{e}") for r in "AB" for e in ("act", "dve", "dve_values")}
        small_loaded = sem("small_loaded")
        x_loaded = sem("x_loaded")
        ident_loaded = sem("ident_loaded")
        par_loaded = sem("par_loaded")
        mem_loaded = sem("mem_loaded")
        p_loaded = sem("p_loaded")
        gf_loaded = sem("gf_loaded")
        prepared = sem("prepared")
        pool_const = sem("pool_const")
        sw_rounded = sem("sw_rounded")
        sw_split = sem("sw_split")
        sq_done = sem("sq_done")
        ms_done = sem("ms_done")
        diag_built = sem("diag_built")
        diag_used = sem("diag_used")
        rstd_done = sem("rstd_done")
        xn_done = sem("xn_done")
        x_new = sem("x_new")
        hi_done = sem("hi_done")
        lo_done = sem("lo_done")
        act_for_pe = sem("act_for_pe")
        act_for_dve = sem("act_for_dve")
        dve_for_pe = sem("dve_for_pe")
        dve_for_act = sem("dve_for_act")
        dve_chain = sem("dve_chain")
        act_chain = sem("act_chain")
        max_done = sem("max_done")
        exp_done = sem("exp_done")
        prob_done = sem("prob_done")
        pt_done = sem("pt_done")
        gn_stat = sem("gn_stat")
        gn_rstd = sem("gn_rstd")
        out_done = sem("out_done")
        out_stored = sem("out_stored")

        def ready(eng, key):
            kind, n = USES.ready[key]
            eng.wait_ge(aux_done if kind == "aux" else w_used, n)

        def is_free(eng, key):
            who, n = USES.freed[key]
            eng.wait_ge(freed[who], n)

        order = {"act": {}, "dve": {}}

        def free(ins, key, eng):
            who, n = USES.freed[key]
            assert who[1].split("_")[0] == eng, key
            order[eng][who] = order[eng].get(who, 0) + 1
            assert order[eng][who] == n, (key, n, order[eng][who])
            ins.then_inc(freed[who], 1)

        def B(key):
            return bank[USES.bank[key]]

        norms = {0: ["g_mem"], 1: ["g_mix0"], 2: ["g_ffn0"], 3: ["g_mix1", "g_kv"], 4: ["g_ffn1"], 5: ["ret_norm"],
                 6: ["ple_norm0"], 7: ["nsa_norm", "kv_norm"], 8: ["ple_norm1"]}
        norm_hi = {0: [MH], 3: [XH, KH], 7: [XH, MH]}
        norm_lo = {0: [ML], 3: [XL, KL], 7: [XL, ML]}
        x_from = {2: "o0", 3: "f0", 4: "o1", 9: "f1", 5: 0, 6: "ro", 7: 2, 8: "no", 10: 6}

        def x_there(eng, n, i, half):
            if n not in x_from:
                return
            if n == 5:
                eng.wait_ge(x_new, i + 1)
            elif isinstance(x_from[n], str):
                is_free(eng, (x_from[n], 2 * i + half))
            else:
                eng.wait_ge(x_new, x_from[n] + 2 * i + half + 1)

        pe_taps = [(b, k) for b in PE_CONV for k in range(CONV)]
        w0 = PCOL["w_dw_a"][0]

        def tap(b, k):
            return par[:, w0 + k * NMB + b:w0 + k * NMB + b + 1]

        block = ctx.enter_context(nc.Block())

        @block.sync
        def _(sp):
            sp.dma_start(x[:, :, :], x_in.rearrange("o (i p) d -> p (o i) d", p=P)).then_inc(x_loaded, 16)
            sp.dma_start(ident_sb[:, :], ident_in).then_inc(ident_loaded, 16)
            sp.dma_start(par[:, :], params).then_inc(par_loaded, 16)

            def load(t):
                if t >= RING:
                    sp.wait_ge(w_split, t - RING + 1)
                sp.dma_start(RAW[:, t % RING, :], wstream[t]).then_inc(w_loaded[t % RING], 16)

            for t in range(RING):
                load(t)
            sp.dma_start(memx, mem_in.rearrange("o (i p) d -> p (o i) d", p=P)).then_inc(mem_loaded, 16)
            sp.dma_start(con[:, :], consts).then_inc(small_loaded, 16)
            sp.dma_start(bfree[:, :], b_f.partition_broadcast(P)).then_inc(small_loaded, 16)
            sp.dma_start(gfree[:, :], g_final.partition_broadcast(P)).then_inc(gf_loaded, 16)
            sp.dma_start(pin, p_in[0].rearrange("o (i p) d -> p (o i) d", p=P)).then_inc(p_loaded, 16)
            for t in range(RING, NT):
                if TILES[t] == ("ro", 0):
                    sp.wait_ge(x_new, 2)
                    sp.dma_start(gfree[:, :], final_norm.partition_broadcast(P)).then_inc(gf_loaded, 16)
                if TILES[t] == ("nq", 3):
                    sp.wait_ge(w_used, TILE[("c1k", 0)] + 1)
                    sp.dma_start(pin, p_in[1].rearrange("o (i p) d -> p (o i) d", p=P)).then_inc(p_loaded, 16)
                load(t)
            for i in range(TT):
                sp.wait_ge(out_done, i + 1)
                sp.dma_start(out[0, i * P:(i + 1) * P, :], xn[:, i, :]).then_inc(out_stored, 16)
            sp.wait_ge(out_stored, 16 * TT)

        @block.gpsimd
        def _(pool):
            ms_a = After(ms_done)
            gn = After(gn_stat)
            nc.gpsimd.memset(mhalf[:, :], -0.5).then_inc(pool_const, 1)
            pool.wait_ge(pool_const, 1)

            def rms(n):
                for i in range(TT):
                    pool.wait_ge(*ms_a.next())
                    nc.gpsimd.tensor_tensor(rstd[:, n, i:i + 1], ms[:, n, i:i + 1], mhalf[:, 0:1], ALU.pow).then_inc(rstd_done, 1)

            for n in (1, 0, 2, 3, 4, 9, 5):
                rms(n)
            for h in range(RH):
                a = 16 + 4 * (h % 2)
                pool.wait_ge(*gn.next())
                nc.gpsimd.tensor_tensor(stat[:, a + 2:a + 4], stat[:, a:a + 2], mhalf[:, :], ALU.pow).then_inc(gn_rstd, 1)
            for n in (6, 7, 8, 10):
                rms(n)

        @block.tensor
        def _(pe):
            tiles, uses = [0], [0]
            xn_a, hi_a, lo_a = After(xn_done), After(hi_done), After(lo_done)
            act_a, dve_a = After(act_for_pe), After(dve_for_pe)
            prob_a, pt_a = After(prob_done), After(pt_done)
            mm = nc.tensor.matmul

            def take(key):
                while BANKS[uses[0]][0] == "complete":
                    uses[0] += 1
                assert BANKS[uses[0]][1] == key, (BANKS[uses[0]], key)
                uses[0] += 1
                if USES.before[key]:
                    who, n = USES.before[key]
                    pe.wait_ge(freed[who], n)
                return B(key)

            def tile(key):
                t = tiles[0]
                assert TILES[t] == key, (TILES[t], key)
                tiles[0] += 1
                pe.wait_ge(w_split, t + 1)
                return WH[:, t % RING, :], WL[:, t % RING, :]

            def three(o, wide, a, b, start, stop):
                (ah, al), (bh, bl) = a, b
                mm(o, ah, bh, start=start, stop=False)
                mm(o, ah, bl, start=False, stop=False)
                return mm(o, al, bh, start=False, stop=stop)

            def parts(n, k, first):
                if n is not None and first and k % 2 == 0:
                    is_free(pe, ("tr", n, k // 2))

            def gemm_t(key, xh, xl, n=None):
                o = take(key)
                wh, wl = tile(key)
                for b in range(2):
                    for k in range(KD):
                        parts(n, k, b == 0)
                        s = slice(k * 256 + b * P, k * 256 + b * P + P)
                        last = three(o[:, b * T:(b + 1) * T], T, (wh[:, s], wl[:, s]), (xh[:, k, :], xl[:, k, :]),
                                     k == 0, k == KD - 1)
                last.then_inc(w_used, 1)

            def gemm_v(key, xh, xl, n=None):
                o = take(key)
                wh, wl = tile(key)
                for i in range(TT):
                    for k in range(KD):
                        parts(n, k, i == 0)
                        s, c = slice(i * P, (i + 1) * P), slice(k * 256, (k + 1) * 256)
                        last = three(o[:, i * 256:(i + 1) * 256], 256, (xh[:, k, s], xl[:, k, s]), (wh[:, c], wl[:, c]),
                                     k == 0, k == KD - 1)
                last.then_inc(w_used, 1)

            def gemm_n(name, xh, xl):
                o = [take((*name, i, "out")) for i in range(TT)]
                for half in range(2):
                    wh, wl = tile((*name, half))
                    for i in range(TT):
                        for k in range(4):
                            kk, s, c = half * 4 + k, slice(i * P, (i + 1) * P), slice(k * 512, (k + 1) * 512)
                            last = three(o[i][:, :], 512, (xh[:, kk, s], xl[:, kk, s]), (wh[:, c], wl[:, c]),
                                         kk == 0, kk == KD - 1)
                    last.then_inc(w_used, 1)

            def gemm_d(key, o, xh, xl, k0, first, end, n=None, early=True):
                wh, wl = tile(key)
                if n is not None:
                    is_free(pe, ("tr", n, k0 // 2))
                for i in range(TT):
                    for k in range(2):
                        for half in range(2):
                            s, c = slice(i * P, (i + 1) * P), slice(k * D + half * 512, k * D + half * 512 + 512)
                            last = three(o[2 * i + half][:, :], 512, (xh[:, k0 + k, s], xl[:, k0 + k, s]),
                                         (wh[:, c], wl[:, c]), first and k == 0, end and k == 1)
                    if i == 0 and end and early:
                        last.then_inc(aux_done, 1)
                last.then_inc(w_used, 1)

            def norm(n):
                o = [take(("tr", n, j)) for j in range(4)]
                for i in range(TT):
                    pe.wait_ge(*xn_a.next())
                    for j in range(4):
                        for kk in range(2):
                            last = nc.tensor.transpose(o[j][:, kk * T + i * P:kk * T + (i + 1) * P],
                                                       xn[:, i, (2 * j + kk) * P:(2 * j + kk + 1) * P], ident)
                        if i == TT - 1:
                            last.then_inc(aux_done, 1)

            def attention(base, units, score, value, between={}):
                n = len(units)
                for s in range(n + 2):
                    if s < n:
                        o = take(("S", base + s))
                        score(units[s], o).then_inc(aux_done, 1)
                    if 0 <= s - 1 < n:
                        o = take(("T", base + s - 1))
                        pe.wait_ge(*prob_a.next())
                        p = prob[:, (s - 1) % 2, :]
                        kind = units[s - 1][0]
                        pieces = ([(0, 0), (256, 128), (128, 256), (384, 384)] if kind == "mem"
                                  else [(0, 0), (128, 128), (256, 256)])
                        for a, b in pieces:
                            last = nc.tensor.transpose(o[:, b:b + P], p[:, a:a + P], ident)
                        last.then_inc(aux_done, 1)
                    if s in between:
                        gemm_t(between[s], *((KH, KL) if between[s][0] == "k1" else (XH, XL)))
                    if 0 <= s - 2 < n:
                        if (s - 2) % 2 == 0:
                            o_val = take(("O", base + s - 2))
                        pe.wait_ge(*pt_a.next())
                        last = value(units[s - 2], o_val, probT[:, (s - 2) % 2, :])
                        if (s - 2) % 2 == 1:
                            last.then_inc(aux_done, 1)

            def score(unit, o):
                kind, h = unit[0], unit[-1]
                r = slice(DH * (h % 2), DH * (h % 2) + DH)
                if kind == "mem":
                    l = unit[1]
                    if l == 1 and h == 0:
                        is_free(pe, ("qm", 1))
                    for i in range(TT):
                        last = mm(o[:, i * T:(i + 1) * T], q_mem[r, h // 2, i * P:(i + 1) * P], mkt[r, l, h // 2, :],
                                  start=True, stop=True)
                    return last
                if h % 4 == 0:
                    is_free(pe, ("q1", h // 4))
                for i in range(TT):
                    a, n = (0, P) if i == 0 else (P, T)
                    t = slice(i * P, (i + 1) * P)
                    mm(o[:, a:a + n], q1[r, h // 2, t], k1[r, h // 2, 0:n], start=True, stop=False)
                    mm(o[:, a:a + n], cumT[0:FOX, 0, t], ident[0:FOX, h:h + 1].to_broadcast([FOX, n]),
                       start=False, stop=False)
                    mm(o[:, a:a + n], ident[0:FOX, h:h + 1].to_broadcast([FOX, P]), cumT[0:FOX, 1, 0:n],
                       start=False, stop=False)
                    last = mm(o[:, a + n - P:a + n], identb[:, :], causb[:, :], start=False, stop=True)
                return last

            def value(unit, o, pt):
                kind, h = unit[0], unit[-1]
                r = slice(DH * (h % 2), DH * (h % 2) + DH)
                if kind == "mem":
                    l = unit[1]
                    for j in range(TT):
                        last = mm(o[r, 0:T], mvv[:, l, j, DH * h:DH * (h + 1)], pt[:, j * T:(j + 1) * T],
                                  start=(j == 0), stop=(j == TT - 1))
                    return last
                mm(o[r, 0:T], v1[:, 0, DH * h:DH * (h + 1)], pt[:, 0:T], start=True, stop=False)
                return mm(o[r, P:T], v1[:, 1, DH * h:DH * (h + 1)], pt[:, T:384], start=False, stop=True)

            def ffn(l):
                o = [take((f"f{l}", i)) for i in range(4)]
                for s in range(FSTEP + 1):
                    if s < FSTEP:
                        gemm_t(("fg", l, s), XH, XL, 2 + 2 * l if s == 0 else None)
                        gemm_t(("fv", l, s), XH, XL)
                    if s:
                        pe.wait_ge(*lo_a.next())
                        gemm_d(("fd", l, s - 1), o, MH, ML, 2 * ((s - 1) % 2), s == 1, s == FSTEP)

            def ple(l):
                o = take(("pt", l))
                pe.wait_ge(p_loaded, 16 * (l + 1))
                for k in range(2):
                    for i in range(TT):
                        last = nc.tensor.transpose(o[:, k * T + i * P:k * T + (i + 1) * P], pin[:, i, k * P:(k + 1) * P], ident)
                last.then_inc(aux_done, 1)
                norm(6 + 2 * l)
                o = [take(("pe", l, i)) for i in range(4)]
                gemm_d(("pe", l), o, PH, PL, 0, True, True, early=False)
                o = [take((f"pg{l}", i)) for i in range(4)]
                for c in range(4):
                    gemm_d((f"pg{l}", c), o, XH, XL, 2 * c, c == 0, c == 3, 6 + 2 * l)

            pe.wait_ge(ident_loaded, 16)
            norm(1)
            for j in range(3):
                gemm_t(("ca", j), XH, XL, 1 if j == 0 else None)
                gemm_t(("cg", j), XH, XL)
            gemm_t(("qm", 0), XH, XL)
            norm(0)
            for l in range(2):
                gemm_t(("mk", l), MH, ML, 0 if l == 0 else None)
                gemm_v(("mv", l), MH, ML)
            pe.wait_ge(*dve_a.next())
            n = 0
            for b in PE_CONV:
                o = take(("cv", b))
                for k in range(CONV):
                    pe.wait_ge(diag_built, n + 1)
                    mm(o[:, 0:T], diag[:, n % DIAGS, :], vpad[:, b, k:k + T], start=(k == 0), stop=(k == CONV - 1))\
                        .then_inc(diag_used if k < CONV - 1 else aux_done, 1)
                    n += 1
            pe.wait_ge(*act_a.next())
            attention(0, [("mem", 0, h) for h in range(4)], score, value)
            pe.wait_ge(small_loaded, 32)
            o = take(("mean",))
            pe.wait_ge(*dve_a.next())
            for b in range(NMB):
                last = mm(o[:, 0:T], ones, conv[:, b, :], start=(b == 0), stop=(b == NMB - 1))
            last.then_inc(aux_done, 1)
            o = take(("var",))
            pe.wait_ge(*act_a.next())
            for b in range(NMB):
                last = mm(o[:, 0:T], ones, lnsq[:, b, :], start=(b == 0), stop=(b == NMB - 1))
            last.then_inc(aux_done, 1)
            o = [take(("o0", i)) for i in range(4)]
            for c in range(4):
                if c < NMB // 2:
                    pe.wait_ge(*lo_a.next())
                gemm_d(("o0", c), o, MH, ML, 2 * c, c == 0, c == 3)
            norm(2)
            ffn(0)
            norm(3)
            for j in range(3):
                gemm_v(("v1", j), KH, KL, 3 if j == 0 else None)
            o = take(("fl",))
            pe.wait_ge(sw_split, 1)
            for i in range(TT):
                for k in range(KD):
                    s, c = slice(i * P, (i + 1) * P), slice(k * FOX, (k + 1) * FOX)
                    last = three(o[:, i * FOX:(i + 1) * FOX], FOX, (KH[:, k, s], KL[:, k, s]), (SWH[:, c], SWL[:, c]),
                                 k == 0, k == KD - 1)
            last.then_inc(aux_done, 1)
            gemm_t(("k1", 0), KH, KL)
            o = take(("cum",))
            pe.wait_ge(*dve_a.next())
            tri = const("tri8").rearrange("p (i t) -> p i t", i=TT)
            for i in range(TT):
                last = mm(o[0:FOX, 0:T], lf[:, 3, i * FOX:(i + 1) * FOX], tri[:, i, :], start=(i == 0), stop=(i == TT - 1))
            last.then_inc(aux_done, 1)
            gemm_t(("q1", 0), XH, XL)
            is_free(pe, ("v1", 2))
            pe.wait_ge(*dve_a.next())
            attention(4, [("fox", h) for h in range(FOX)] + [("mem", 1, h) for h in range(4)], score, value, FOX_TILES)
            o = [take(("o1", i)) for i in range(4)]
            pe.wait_ge(*lo_a.next())
            for c in range(4):
                gemm_d(("o1", c), o, MH, ML, 2 * c, c == 0, c == 3)
            norm(4)
            ffn(1)
            norm(5)
            for h in range(RH):
                gemm_t(("rq", h), XH, XL, 5 if h == 0 else None)
                gemm_t(("rk", h), XH, XL)

            def ret_turn(h):
                pe.wait_ge(*dve_a.next())
                for j in range(2):
                    o = take(("ry", h, j))
                    for kk in range(2):
                        for i in range(TT):
                            c = (2 * j + kk) * P
                            last = nc.tensor.transpose(o[:, kk * T + i * P:kk * T + (i + 1) * P], ry[:, i, c:c + P], ident)
                    last.then_inc(aux_done, 1)

            for h in range(RH):
                gemm_n(("rv", h), XH, XL)
                gemm_n(("rg", h), XH, XL)
                o = take(("rs", h))
                if h == 0:
                    pe.wait_ge(*dve_a.next())
                for m in range(TT):
                    for c in range(2):
                        last = mm(o[:, m * T:m * T + T - m * P], kr[:, h, c * T + m * P:c * T + (m + 1) * P],
                                  qr[:, h, c * T + m * P:(c + 1) * T], start=(c == 0), stop=(c == 1))
                last.then_inc(aux_done, 1)
                is_free(pe, ("rs", h))
                is_free(pe, ("rv", h, 1, "out"))
                for i in range(TT):
                    o = take(("ro", h, i))
                    for m in range(i + 1):
                        a = m * T + (i - m) * P
                        last = mm(o[:, :], sdt[:, h % 2, a:a + P], rv[:, m, :], start=(m == 0), stop=(m == i))
                    last.then_inc(aux_done, 1)
                if h:
                    ret_turn(h - 1)
            ret_turn(RH - 1)
            o = [take(("ro", i)) for i in range(4)]
            is_free(pe, ("ry", RH - 1, 1))
            for c in range(8):
                gemm_d(("ro", c), o, MH, ML, 2 * c, c == 0, c == 7)
            ple(0)
            norm(7)
            for n in ("kc", "vc", "ks", "kw"):
                for j in range(2):
                    gemm_t((n, j), MH, ML, 7 if (n, j) == ("kc", 0) else None)
            for n in ("vs", "vw"):
                gemm_n((n,), MH, ML)
            o = take(("bg",))
            for i in range(TT):
                for k in range(KD):
                    s, c = slice(i * P, (i + 1) * P), slice(KD * FOX + k * 48, KD * FOX + (k + 1) * 48)
                    last = three(o[:, i * 48:(i + 1) * 48], 48, (XH[:, k, s], XL[:, k, s]), (SWH[:, c], SWL[:, c]),
                                 k == 0, k == KD - 1)
            last.then_inc(aux_done, 1)
            bh = MH[:, :, :].rearrange("p a b -> p (a b)").rearrange("p (l c) -> p l c", c=P)
            bl = ML[:, :, :].rearrange("p a b -> p (a b)").rearrange("p (l c) -> p l c", c=P)
            for n, u in (("c1k", "hk"), ("c1v", "hv")):
                o = take((u,))
                for at, j in enumerate(CMP_ORDER):
                    wh, wl = tile((n, j))
                    if n == "c1k" and at % 2 == 0:
                        pe.wait_ge(*lo_a.next())
                    for i in range(8):
                        l, c = 8 * j + i, slice(i * 256, (i + 1) * 256)
                        last = three(o[:, 0:256], 256, (bh[:, l, :], bl[:, l, :]), (wh[:, c], wl[:, c]),
                                     at == 0 and i == 0, at == 3 and i == 7)
                    last.then_inc(w_used, 1)
            gemm_t(("nq", 0), XH, XL)
            gemm_t(("ng", 0), XH, XL)
            o = take(("ht",))
            pe.wait_ge(*dve_a.next())
            for j in range(2):
                last = nc.tensor.transpose(o[:, j * P:(j + 1) * P], hs[:, j * P:(j + 1) * P], ident)
            last.then_inc(aux_done, 1)
            o = take(("kct",))
            is_free(pe, ("ht",))
            w2k, w2v = col("w2_k"), col("w2_v")
            for j in range(2):
                last = mm(o[:, 0:64], w2k[:, j * P:(j + 1) * P], hT[:, j, 0:64], start=(j == 0), stop=(j == 1))
            last.then_inc(aux_done, 1)
            o = take(("vcm",))
            for g in range(NSA_G):
                for j in range(2):
                    last = mm(o[0:CMP_S, g * P:(g + 1) * P], hT[:, j, 64 + g * CMP_S:64 + (g + 1) * CMP_S],
                              w2v[:, j * P:(j + 1) * P], start=(j == 0), stop=(j == 1))
            last.then_inc(aux_done, 1)
            is_free(pe, ("vcm",))
            for s in range(NSA_H + 1):
                if s < NSA_H:
                    h, g, qh = s, s // 4, qb[:, (s // 2) % 2, (s % 2) * T:(s % 2) * T + T]
                    oS, oW = take(("Ss", s)), take(("Sw", s))
                    is_free(pe, ("nq", s // 2))
                    for i in range(TT):
                        a, n = (0, P) if i == 0 else (P, T)
                        mm(oS[:, a:a + n], qh[:, i * P:(i + 1) * P], ksT[:, g, 0:n], start=True, stop=False)
                        mm(oS[:, a + n - P:a + n], identb[:, :], causb[:, :], start=False, stop=True)
                    for i in range(TT):
                        c = slice(384 + i * CMP_S, 384 + (i + 1) * CMP_S)
                        mm(oS[:, c], qh[:, i * P:(i + 1) * P], kct[:, g * CMP_S:(g + 1) * CMP_S], start=True, stop=False)
                        last = mm(oS[:, c], identb[:, :], cmpb[:, i * CMP_S:(i + 1) * CMP_S], start=False, stop=True)
                    last.then_inc(aux_done, 1)
                    for i in range(TT):
                        a, n = (0, P) if i == 0 else (P, T)
                        mm(oW[:, a:a + n], qh[:, i * P:(i + 1) * P], kwT[:, g, 0:n], start=True, stop=False)
                        last = mm(oW[:, a + n - P:a + n], identb[:, :], causb[:, :], start=False, stop=True)
                    last.then_inc(aux_done, 1)
                if 0 <= s - 1 < NSA_H:
                    oS, oW, e = take(("Ts", s - 1)), take(("Tw", s - 1)), (s - 1) % 2
                    pe.wait_ge(*prob_a.next())
                    for o, p, i in ((oS, pS, 0), (oW, pW, 1)):
                        for a in range(3):
                            nc.tensor.transpose(o[:, a * P:(a + 1) * P], p[:, e, a * P:(a + 1) * P], ident)
                        last = nc.tensor.transpose(o[0:CMP_S, 384:512], pC[:, e, i * CMP_S:(i + 1) * CMP_S], ident)
                        last.then_inc(aux_done, 1)
                if s // 2 + 1 < 8:
                    gemm_t((("nq", "ng")[s % 2], s // 2 + 1), XH, XL)
                if s:
                    g = (s - 1) // 4
                    o = take(("On", s - 1))
                    is_free(pe, ("Ts", s - 1))
                    is_free(pe, ("Tw", s - 1))
                    mm(o[:, 0:T], vcm[0:CMP_S, g, :], ptC[0:CMP_S, :], start=True, stop=False)
                    for n, (p, v) in enumerate(((ptS, vs), (ptW, vw))):
                        mm(o[:, 0:T], v[:, 0, g * P:(g + 1) * P], p[:, 0:T], start=False, stop=False)
                        last = mm(o[:, P:T], v[:, 1, g * P:(g + 1) * P], p[:, T:384], start=False, stop=(n == 1))
                    last.then_inc(aux_done, 1)
            o = [take(("no", i)) for i in range(4)]
            pe.wait_ge(*lo_a.next())
            for c in range(8):
                gemm_d(("no", c), o, MH, ML, 2 * c, c == 0, c == 7)
            ple(1)
            assert tiles[0] == NT and all(u[0] == "complete" for u in BANKS[uses[0]:])

        @block.scalar
        def _(act):
            n_round, n_sq, chain = [0], [0], [0]
            act_fn = nc.scalar.activation
            max_a, dve_a = After(max_done), After(dve_for_act)

            def upto(key):
                while n_round[0] < min(TILE[key] + RING, NT):
                    t = n_round[0]
                    n_round[0] += 1
                    act.wait_ge(w_loaded[t % RING], 16 * (t // RING + 1))
                    if t >= RING:
                        act.wait_ge(w_used, t - RING + 1)
                    act_fn(WH[:, t % RING, :], RAW[:, t % RING, :], ACT.Copy).then_inc(w_rounded, 1)

            def link(ins):
                chain[0] += 1
                ins.then_inc(act_chain, 1)

            def sync():
                act.wait_ge(act_chain, chain[0])

            def squares(n, src):
                for i in range(TT):
                    for half in range(2):
                        c = slice(half * 512, half * 512 + 512)
                        x_there(act, n, i, half)
                        if n_sq[0] > 1:
                            act.wait_ge(sq_done, n_sq[0] - 1)
                        n_sq[0] += 1
                        act_fn(junk[:, c], src[:, i, c], ACT.Square, scale=D ** -0.5,
                               accum_out=ss[:, n, 2 * i + half:2 * i + half + 1]).then_inc(sq_done, 1)

            def high_parts(n):
                for j in range(4):
                    ready(act, ("tr", n, j))
                    for kk in range(2):
                        k = 2 * j + kk
                        for dst, g in zip(norm_hi.get(n, [XH]), norms[n]):
                            act_fn(dst[:, k, :], B(("tr", n, j))[:, kk * T:(kk + 1) * T], ACT.Copy,
                                   scale=col(g, k)).then_inc(hi_done, 1)

            def norm(n, src):
                squares(n, src)
                high_parts(n)

            def projected(key, dst):
                upto(key)
                ready(act, key)
                free(act_fn(dst, B(key)[:, :].rearrange("p (b t) -> p b t", b=2), ACT.Copy), key, "act")

            def attention(base, units, blocks_at, between={}):
                n = len(units)
                for s in range(n + 3):
                    if s >= 3 and (s - 3) % 2 == 1:
                        m = s - 4
                        ready(act, ("O", base + m))
                        act_fn(MH[:, blocks_at[m // 2], :], B(("O", base + m))[:, 0:T], ACT.Copy).then_inc(hi_done, 1)
                    if s < n:
                        e, kind = s % 2, units[s][0]
                        segs = [(0, T), (T, T)] if kind == "mem" else [(0, P), (P, T)]
                        act.wait_ge(*max_a.next())
                        for i, (a, w) in enumerate(segs):
                            ins = act_fn(prob[:, e, a:a + w], B(("S", base + s))[:, a:a + w], ACT.Exp,
                                         bias=stat[:, 2 * e + i:2 * e + i + 1], scale=DH ** -0.5,
                                         accum_out=stat[:, 4 + 2 * e + i:5 + 2 * e + i])
                            if i == 0:
                                ins.then_inc(exp_done, 1)
                        free(ins, ("S", base + s), "act")
                    if s - 1 in between:
                        name, j = between[s - 1]
                        projected((name, j), q_mem if name == "qm" else {"k1": k1, "q1": q1}[name][:, 2 * j:2 * j + 2, :])

            def ffn(l):
                for s in range(FSTEP):
                    e = s % 2
                    for q, name in enumerate(("fg", "fv")):
                        upto((name, l, s))
                        ready(act, (name, l, s))
                        for b in range(2):
                            f = q * 22 + 2 * s + b
                            act_fn(fy[:, e, (2 * q + b) * T:(2 * q + b + 1) * T], B((name, l, s))[:, b * T:(b + 1) * T],
                                   ACT.Identity, bias=col(f"b_dw_f{l}", f), scale=col(f"w_dw_f{l}", 2 * 44 + f)).then_inc(act_for_dve, 1)
                        if q == 0:
                            act.wait_ge(*dve_a.next())
                            act_fn(fth[:, e, :], fy[:, e, 0:2 * T], ACT.Tanh, scale=0.5).then_inc(act_for_dve, 1)
                    upto(("fd", l, s - 1) if s else ("fv", l, 0))
                    act.wait_ge(*dve_a.next())
                    act_fn(MH[:, 2 * e:2 * e + 2, :], fa[:, e, :].rearrange("p (b t) -> p b t", b=2), ACT.Copy).then_inc(hi_done, 1)

            def ple(l):
                squares(6 + 2 * l, x)
                ready(act, ("pt", l))
                act_fn(PH[:, :, :], B(("pt", l))[:, :].rearrange("p (k t) -> p k t", k=2), ACT.Copy).then_inc(hi_done, 1)
                high_parts(6 + 2 * l)
                upto(("pe", l))
                for c in range(4):
                    upto((f"pg{l}", c))
                for i in range(4):
                    ready(act, (f"pg{l}", i))
                    act_fn(pth[:, i, :], B((f"pg{l}", i))[:, :], ACT.Tanh, scale=0.5).then_inc(act_for_dve, 1)

            act.wait_ge(x_loaded, 16)
            squares(1, x)
            upto(TILES[0])
            act.wait_ge(par_loaded, 16)
            high_parts(1)
            act.wait_ge(mem_loaded, 16)
            squares(0, memx)
            sw = PCOL["w_f"][0]
            act_fn(SWH[:, :], par[:, sw:sw + KD * (FOX + 48)], ACT.Copy).then_inc(sw_rounded, 1)
            act.wait_ge(prepared, 1)
            for j in range(3):
                upto(("ca", j))
                ready(act, ("ca", j))
                if j:
                    act.wait_ge(*dve_a.next())
                for b in range(2):
                    ins = act_fn(glu_a[:, b, :], B(("ca", j))[:, b * T:(b + 1) * T], ACT.Identity, scale=0.5,
                                 bias=hbglu[:, 2 * j + b:2 * j + b + 1])
                free(ins, ("ca", j), "act")
                upto(("cg", j))
                ready(act, ("cg", j))
                for b in range(2):
                    ins = act_fn(glu_t[:, b, :], B(("cg", j))[:, b * T:(b + 1) * T], ACT.Tanh, scale=0.5,
                                 bias=hbglu[:, NMB + 2 * j + b:NMB + 2 * j + b + 1])
                free(ins, ("cg", j), "act")
                act.drain().then_inc(act_for_dve, 1)
            projected(("qm", 0), q_mem)
            high_parts(0)
            for l in range(2):
                projected(("mk", l), mkt[:, l, :, :])
                projected(("mv", l), mvv[:, l, :, :])
            for n, (b, k) in enumerate(pe_taps):
                if n >= DIAGS:
                    old_b, old_k = pe_taps[n - DIAGS]
                    if old_k == CONV - 1:
                        ready(act, ("cv", old_b))
                    else:
                        act.wait_ge(diag_used, n - DIAGS + 1 - PE_CONV.index(old_b))
                act_fn(diag[:, n % DIAGS, :], ident, ACT.Copy, scale=tap(b, k)).then_inc(diag_built, 1)
            act.drain().then_inc(act_for_pe, 1)
            attention(0, [("mem", 0, h) for h in range(4)], [NMB, NMB + 1])
            act.wait_ge(*dve_a.next())
            act_fn(lnsq, conv, ACT.Square).then_inc(act_for_pe, 1)
            act.wait_ge(*dve_a.next())
            act_fn(rs_ln, rs_ln, ACT.Sqrt).then_inc(act_for_dve, 1)
            for pair in range(NMB // 2):
                act.wait_ge(*dve_a.next())
                for b in (2 * pair, 2 * pair + 1):
                    link(act_fn(z[:, b, :], conv[:, b, :], ACT.Identity, scale=col("ln_g", b), bias=col("ln_b", b)))
                sync()
                c = slice(2 * pair, 2 * pair + 2)
                act_fn(lnsq[:, c, :], z[:, c, :], ACT.Tanh, scale=0.5).then_inc(act_for_dve, 1)
            for pair in range(NMB // 2):
                act.wait_ge(*dve_a.next())
                c = slice(2 * pair, 2 * pair + 2)
                act_fn(MH[:, c, :], conv[:, c, :], ACT.Copy, scale=0.5).then_inc(hi_done, 1)
            for c in range(4):
                upto(("o0", c))
            norm(2, x)
            ffn(0)
            upto(("fd", 0, FSTEP - 1))
            norm(3, x)
            for j in range(3):
                projected(("v1", j), v1[:, :, j * 256:(j + 1) * 256])
            act.wait_ge(*dve_a.next())
            link(act_fn(lf[:, 1, :], lf[:, 1, :], ACT.Exp))
            sync()
            act_fn(lf[:, 2, :], lf[:, 1, :], ACT.Ln, bias=1.0).then_inc(act_for_dve, 1)
            projected(("k1", 0), k1[:, 0:2, :])
            projected(("q1", 0), q1[:, 0:2, :])
            attention(4, [("fox", h) for h in range(FOX)] + [("mem", 1, h) for h in range(4)],
                      list(range(NMB)) + [NMB, NMB + 1], FOX_TILES)
            for c in range(4):
                upto(("o1", c))
            norm(4, x)
            ffn(1)
            upto(("fd", 1, FSTEP - 1))
            squares(9, x)
            norm(5, x)
            for h in range(RH):
                upto(("rq", h))
                upto(("rk", h))

            def ret_out(h):
                for j in range(2):
                    ready(act, ("ry", h, j))
                    for kk in range(2):
                        f = 4 * h + 2 * j + kk
                        act_fn(MH[:, f, :], B(("ry", h, j))[:, kk * T:(kk + 1) * T], ACT.Copy, scale=hgn[:, f:f + 1]).then_inc(hi_done, 1)

            for h in range(RH):
                upto(("rv", h, 1))
                for i in range(TT):
                    ready(act, ("rv", h, i, "out"))
                    free(act_fn(rv[:, i, :], B(("rv", h, i, "out"))[:, :], ACT.Copy), ("rv", h, i, "out"), "act")
                upto(("rg", h, 1))
                for i in range(TT):
                    ready(act, ("rg", h, i, "out"))
                    act_fn(rth[:, i, :], B(("rg", h, i, "out"))[:, :], ACT.Tanh, scale=0.5).then_inc(act_for_dve, 1)
                if h:
                    ret_out(h - 1)
            ret_out(RH - 1)
            for c in range(8):
                upto(("ro", c))
            ple(0)
            norm(7, x)
            blocks_flat = blocks.rearrange("p l c -> p (l c)").rearrange("p (a b) -> p a b", a=16)
            for n, dst in (("kc", kvc[:, 0:4, :]), ("vc", kvc[:, 4:8, :]), ("ks", ksT), ("kw", kwT)):
                for j in range(2):
                    projected((n, j), dst[:, 2 * j:2 * j + 2, :])
                    if (n, j) == ("kw", 0):
                        act.wait_ge(*dve_a.next())
                        act_fn(MH[:, 8:16, :], blocks_flat[:, 8:16, :], ACT.Copy).then_inc(hi_done, 1)
            for n, dst in (("vs", vs), ("vw", vw)):
                upto((n, 0))
                upto((n, 1))
                for i in range(TT):
                    ready(act, (n, i, "out"))
                    free(act_fn(dst[:, i, :], B((n, i, "out"))[:, :], ACT.Copy), (n, i, "out"), "act")
            act.wait_ge(*dve_a.next())
            act_fn(MH[:, 0:8, :], blocks_flat[:, 0:8, :], ACT.Copy).then_inc(hi_done, 1)
            ready(act, ("bg",))
            free(act_fn(g3.rearrange("p i c -> p (i c)"), B(("bg",))[:, 0:TT * 48], ACT.Tanh, scale=0.5), ("bg",), "act")
            act.drain().then_inc(act_for_dve, 1)
            for n in ("c1k", "c1v"):
                for j in CMP_ORDER[:3]:
                    upto((n, j))
            for n, r in (("hk", slice(0, 64)), ("hv", slice(64, P))):
                ready(act, (n,))
                if n == "hv":
                    upto(("c1v", CMP_ORDER[-1]))
                free(act_fn(hx[r, :], B((n,))[r, 0:256], ACT.Copy), (n,), "act")
            is_free(act, ("hv",))
            act_fn(hs, hx, ACT.Square).then_inc(act_for_dve, 1)
            act.wait_ge(*dve_a.next())
            act_fn(hth, hs, ACT.Tanh, scale=GELU_C).then_inc(act_for_dve, 1)

            def queries(t):
                ready(act, ("nq", t))
                free(act_fn(qb[:, t % 2, :], B(("nq", t))[:, :], ACT.Copy), ("nq", t), "act")

            def gate(t):
                ready(act, ("ng", t))
                act_fn(nth, B(("ng", t))[:, :], ACT.Tanh, scale=0.5).then_inc(act_for_dve, 1)

            upto(("ng", 0))
            queries(0)
            gate(0)
            ready(act, ("ht",))
            free(act_fn(hT.rearrange("p j c -> p (j c)"), B(("ht",))[:, 0:2 * P], ACT.Copy, scale=0.5), ("ht",), "act")
            ready(act, ("kct",))
            free(act_fn(kct, B(("kct",))[:, 0:64], ACT.Copy), ("kct",), "act")
            ready(act, ("vcm",))
            free(act_fn(vcm[0:CMP_S, :, :].rearrange("p g c -> p (g c)"), B(("vcm",))[0:CMP_S, :], ACT.Copy), ("vcm",), "act")

            for s in range(NSA_H + 2):
                if s >= 2:
                    act.wait_ge(*dve_a.next())
                    act_fn(MH[:, s - 2, :], om[:, s % 2, :], ACT.Copy).then_inc(hi_done, 1)
                if s and (s + 1) // 2 < 8:
                    (gate, queries)[s % 2]((s + 1) // 2)
                if s < NSA_H:
                    e = s % 2
                    act.wait_ge(*max_a.next())
                    for br, (dst, name) in enumerate(((pC, "Ss"), (pS, "Ss"), (pW, "Sw"))):
                        for i in range(TT):
                            if br == 0:
                                a, b, w = 384 + i * CMP_S, i * CMP_S, CMP_S
                            else:
                                a, b, w = (0, 0, P) if i == 0 else (P, P, T)
                            c = 8 * e + 2 * br + i
                            ins = act_fn(dst[:, e, b:b + w], B((name, s))[:, a:a + w], ACT.Exp, bias=stat[:, c:c + 1],
                                         scale=P ** -0.5, accum_out=stat[:, 16 + c:17 + c])
                        if br == 1:
                            free(ins, ("Ss", s), "act")
                    free(ins, ("Sw", s), "act")
                if 0 <= s - 1 < NSA_H:
                    o = B(("Tw", s - 1))
                    ready(act, ("Tw", s - 1))
                    if s > 1:
                        ready(act, ("On", s - 2))
                    link(act_fn(ptW, o[:, 0:384], ACT.Copy))
                    free(act_fn(ptC[0:CMP_S, P:T], o[0:CMP_S, 384:512], ACT.Copy), ("Tw", s - 1), "act")
                if s and (s + 1) // 2 < 8:
                    upto((("ng", "nq")[s % 2], (s + 1) // 2))
            for c in range(8):
                upto(("no", c))
            ple(1)
            squares(10, x)

        @block.vector
        def _(dve):
            n_split, chain = [0], [0]
            hi_a, act_a, rstd_a, sq_a = After(hi_done), After(act_for_dve), After(rstd_done), After(sq_done)
            gn_a, gf_a = After(gn_rstd), After(gf_loaded)
            tt, ts, stt, copy = nc.vector.tensor_tensor, nc.vector.tensor_scalar, nc.vector.scalar_tensor_tensor, nc.vector.tensor_copy

            def upto(key):
                while n_split[0] < min(TILE[key] + RING, NT):
                    t = n_split[0]
                    n_split[0] += 1
                    dve.wait_ge(w_rounded, t + 1)
                    tt(WL[:, t % RING, :], RAW[:, t % RING, :], WH[:, t % RING, :].bitcast(F32), ALU.subtract).then_inc(w_split, 1)

            def link(ins):
                chain[0] += 1
                ins.then_inc(dve_chain, 1)

            def sync():
                dve.wait_ge(dve_chain, chain[0])

            def add(key, i):
                for half in range(2):
                    c = slice(half * 512, half * 512 + 512)
                    ready(dve, (key, 2 * i + half))
                    free(tt(x[:, i, c], B((key, 2 * i + half))[:, :], x[:, i, c], ALU.add), (key, 2 * i + half), "dve")

            def mean_square(n, i):
                dve.wait_ge(*sq_a.next(2))
                stt(ms[:, n, i:i + 1], ss[:, n, 2 * i:2 * i + 1], RMS_EPS, ss[:, n, 2 * i + 1:2 * i + 2],
                    ALU.add, ALU.add).then_inc(ms_done, 1)

            def normed(n, src, scaled=None):
                if scaled is None:
                    def scaled(i):
                        ts(xn[:, i, :], src[:, i, :], rstd[:, n, i:i + 1], None, ALU.mult).then_inc(xn_done, 1)
                key = x_from.get(n)
                if isinstance(key, str):
                    add(key, 0)
                mean_square(n, 0)
                if isinstance(key, str):
                    add(key, 1)
                for i in range(TT):
                    dve.wait_ge(*rstd_a.next())
                    x_there(dve, n, i, 1)
                    scaled(i)
                    if i == 0:
                        mean_square(n, 1)

            def low_parts(n):
                for j in range(4):
                    dve.wait_ge(*hi_a.next(2 * len(norms[n])))
                    for kk in range(2):
                        k = 2 * j + kk
                        for dst, hi, g in zip(norm_lo.get(n, [XL]), norm_hi.get(n, [XH]), norms[n]):
                            ins = stt(dst[:, k, :], B(("tr", n, j))[:, kk * T:(kk + 1) * T], col(g, k),
                                      hi[:, k, :].bitcast(F32), ALU.mult, ALU.subtract)
                    free(ins, ("tr", n, j), "dve")

            def norm(n, src):
                normed(n, src)
                low_parts(n)

            def attention(base, units, blocks_at, between={}):
                n = len(units)
                for s in range(n + 3):
                    if 0 <= s - 2 < n:
                        w = 512 if units[s - 2][0] == "mem" else 384
                        ready(dve, ("T", base + s - 2))
                        copy(probT[:, (s - 2) % 2, 0:w], B(("T", base + s - 2))[:, 0:w]).then_inc(pt_done, 1)
                        free(dve.drain(), ("T", base + s - 2), "dve")
                    if s >= 3 and (s - 3) % 2 == 1:
                        m = s - 4
                        dve.wait_ge(*hi_a.next())
                        b = blocks_at[m // 2]
                        free(tt(ML[:, b, :], B(("O", base + m))[:, 0:T], MH[:, b, :].bitcast(F32), ALU.subtract),
                             ("O", base + m), "dve")
                    if 0 <= s - 1 < n:
                        e, kind = (s - 1) % 2, units[s - 1][0]
                        segs = [(0, T), (T, T)] if kind == "mem" else [(0, P), (P, T)]
                        is_free(dve, ("S", base + s - 1))
                        link(nc.vector.reciprocal(stat[:, 12 + 2 * e:14 + 2 * e], stat[:, 4 + 2 * e:6 + 2 * e]))
                        sync()
                        for i, (a, w) in enumerate(segs):
                            ins = ts(prob[:, e, a:a + w], prob[:, e, a:a + w], stat[:, 12 + 2 * e + i:13 + 2 * e + i], None, ALU.mult)
                        ins.then_inc(prob_done, 1)
                    if s < n:
                        e, kind = s % 2, units[s][0]
                        ready(dve, ("S", base + s))
                        o = B(("S", base + s))
                        mx = stat[:, 8 + 2 * e:10 + 2 * e]
                        if kind == "mem":
                            link(nc.vector.tensor_reduce(mx, o[:, :].rearrange("p (i k) -> p i k", i=2), AX_X, ALU.max))
                        else:
                            link(nc.vector.tensor_reduce(mx[:, 0:1], o[:, 0:P], AX_X, ALU.max))
                            link(nc.vector.tensor_reduce(mx[:, 1:2], o[:, P:384], AX_X, ALU.max))
                        sync()
                        ts(stat[:, 2 * e:2 * e + 2], mx, -DH ** -0.5, None, ALU.mult).then_inc(max_done, 1)
                    if s - 1 in between:
                        upto(between[s - 1])

            def low_signal():
                dve.drain().then_inc(lo_done, 1)

            def ffn(l):
                for s in range(FSTEP):
                    e = s % 2
                    y = fy[:, e, :].rearrange("p (b t) -> p b t", b=4)
                    for q, name in enumerate(("fg", "fv")):
                        upto((name, l, s))
                        dve.wait_ge(*act_a.next(2))
                        for b in range(2):
                            f = q * 22 + 2 * s + b
                            u, yy = B((name, l, s))[:, b * T:(b + 1) * T], y[:, 2 * q + b, :]
                            link(stt(yy[:, 1:T], u[:, 0:T - 1], col(f"w_dw_f{l}", 44 + f), yy[:, 1:T], ALU.mult, ALU.add))
                        sync()
                        for b in range(2):
                            f = q * 22 + 2 * s + b
                            u, yy = B((name, l, s))[:, b * T:(b + 1) * T], y[:, 2 * q + b, :]
                            ins = stt(yy[:, 2:T], u[:, 0:T - 2], col(f"w_dw_f{l}", f), yy[:, 2:T], ALU.mult, ALU.add)
                            if b == 0:
                                link(ins)
                        free(ins, (name, l, s), "dve")
                        is_free(dve, (name, l, s))
                        if q == 0:
                            dve.drain().then_inc(dve_for_act, 1)
                            dve.wait_ge(*act_a.next())
                            link(stt(fth[:, e, :], fth[:, e, :], 1.0, fy[:, e, 0:2 * T], ALU.add, ALU.mult))
                    sync()
                    stt(fa[:, e, :], fth[:, e, :], 0.5, fy[:, e, 2 * T:4 * T], ALU.mult, ALU.mult).then_inc(dve_for_act, 1)
                    upto(("fd", l, s - 1) if s else ("fv", l, 0))
                    dve.wait_ge(*hi_a.next())
                    tt(ML[:, 2 * e:2 * e + 2, :], fa[:, e, :].rearrange("p (b t) -> p b t", b=2),
                       MH[:, 2 * e:2 * e + 2, :].bitcast(F32), ALU.subtract).then_inc(lo_done, 1)
                upto(("fd", l, FSTEP - 1))

            def ple(l):
                normed(6 + 2 * l, x)
                dve.wait_ge(*hi_a.next())
                free(tt(PL[:, :, :], B(("pt", l))[:, :].rearrange("p (k t) -> p k t", k=2), PH[:, :, :].bitcast(F32), ALU.subtract),
                     ("pt", l), "dve")
                low_parts(6 + 2 * l)
                for c in range(4):
                    upto((f"pg{l}", c))
                for i in range(4):
                    dve.wait_ge(*act_a.next())
                    ready(dve, ("pe", l, i))
                    free(stt(pth[:, i, :], pth[:, i, :], 1.0, B(("pe", l, i))[:, :], ALU.add, ALU.mult), ("pe", l, i), "dve")
                    is_free(dve, ("pe", l, i))
                    c = slice((i % 2) * 512, (i % 2) * 512 + 512)
                    stt(x[:, i // 2, c], pth[:, i, :], 0.5, x[:, i // 2, c], ALU.mult, ALU.add).then_inc(x_new, 1)
                    free(dve.drain(), (f"pg{l}", i), "dve")

            first = [(b, i) for i in range(CONV // 2) for b in (0, 1)]
            both = [(b, CONV // 2 * (b < 2) + i) for i in range(CONV) for b in range(4) if CONV // 2 * (b < 2) + i < CONV]
            dve_taps, n_tap, last_of, glu_at = first + both, [0], {}, {}

            def taps(count):
                for _ in range(count):
                    if n_tap[0] == len(dve_taps):
                        return
                    b, i = dve_taps[n_tap[0]]
                    if b // 2 not in glu_at:
                        return
                    n_tap[0] += 1
                    dve.wait_ge(dve_chain, last_of.get(b, glu_at[b // 2]))
                    if i == 0:
                        link(ts(conv[:, b, :], vpad[:, b, CONV - 1:CONV - 1 + T], tap(b, CONV - 1), col("b_dw_a", b), ALU.mult, ALU.add))
                    else:
                        link(stt(conv[:, b, :], vpad[:, b, i - 1:i - 1 + T], tap(b, i - 1), conv[:, b, :], ALU.mult, ALU.add))
                    last_of[b] = chain[0]

            dve.wait_ge(ident_loaded, 16)
            link(copy(identb[:, :], ident))
            link(nc.vector.memset(vpad[:, :, 0:CONV - 1], 0.0))
            normed(1, x)
            upto(TILES[0])
            dve.wait_ge(par_loaded, 16)
            link(ts(hbglu[:, :], col("b_glu"), 0.5, None, ALU.mult))
            link(ts(hgn[:, :], col("ret_gn"), 0.5, None, ALU.mult))
            sync()
            dve.drain().then_inc(prepared, 1)
            low_parts(1)
            for j in range(3):
                upto(("ca", j))
                taps(8)
                upto(("cg", j))
                dve.wait_ge(*act_a.next())
                ins = stt(vpad[:, 2 * j:2 * j + 2, CONV - 1:CONV - 1 + T], glu_t, 1.0, glu_a, ALU.add, ALU.mult)
                if j < 2:
                    link(ins)
                    glu_at[j] = chain[0]
                    dve.drain().then_inc(dve_for_act, 1)
                else:
                    ins.then_inc(dve_for_pe, 1)
                if j == 0:
                    normed(0, memx)
                taps(8)
            upto(("qm", 0))
            taps(8)
            low_parts(0)
            for l in range(2):
                for n in ("mk", "mv"):
                    upto((n, l))
                    taps(8)
            dve.wait_ge(sw_rounded, 1)
            sw = PCOL["w_f"][0]
            tt(SWL[:, :], par[:, sw:sw + KD * (FOX + 48)], SWH[:, :].bitcast(F32), ALU.subtract).then_inc(sw_split, 1)
            taps(4 * CONV)
            for b in PE_CONV:
                ready(dve, ("cv", b))
                free(ts(conv[:, b, :], B(("cv", b))[:, 0:T], col("b_dw_a", b), None, ALU.add), ("cv", b), "dve")
            attention(0, [("mem", 0, h) for h in range(4)], [NMB, NMB + 1])
            dve.wait_ge(small_loaded, 32)
            link(copy(causb[:, :], const("causal")))
            link(copy(cmpb[:, :], const("cmpmask")))
            sync()
            dve.drain().then_inc(dve_for_pe, 1)
            ready(dve, ("mean",))
            tt(conv, conv, B(("mean",))[:, 0:T].unsqueeze(1).to_broadcast([P, NMB, T]), ALU.subtract).then_inc(dve_for_act, 1)
            free(dve.drain(), ("mean",), "dve")
            ready(dve, ("var",))
            ts(rs_ln, B(("var",))[:, 0:T], LN_EPS, None, ALU.add).then_inc(dve_for_act, 1)
            free(dve.drain(), ("var",), "dve")
            dve.wait_ge(*act_a.next())
            link(nc.vector.reciprocal(rs_ln, rs_ln))
            sync()
            pairs = [slice(2 * p, 2 * p + 2) for p in range(NMB // 2)]
            for c in pairs:
                tt(conv[:, c, :], conv[:, c, :], rs_ln.unsqueeze(1).to_broadcast([P, 2, T]), ALU.mult).then_inc(dve_for_act, 1)
            for c in pairs:
                dve.wait_ge(*act_a.next())
                stt(conv[:, c, :], lnsq[:, c, :], 1.0, z[:, c, :], ALU.add, ALU.mult).then_inc(dve_for_act, 1)
            for c in pairs:
                dve.wait_ge(*hi_a.next())
                link(stt(ML[:, c, :], conv[:, c, :], 0.5, MH[:, c, :].bitcast(F32), ALU.mult, ALU.subtract))
                sync()
                low_signal()
            for c in range(4):
                upto(("o0", c))
            norm(2, x)
            ffn(0)
            norm(3, x)
            for j in range(3):
                upto(("v1", j))
            ready(dve, ("fl",))
            zf, az = lf[:, 0, :], lf[:, 1, :]
            free(tt(zf.rearrange("p (i h) -> p i h", i=TT), B(("fl",))[:, 0:TT * FOX].rearrange("p (i h) -> p i h", i=TT),
                    bfree[:, :].unsqueeze(1).to_broadcast([P, TT, FOX]), ALU.add), ("fl",), "dve")
            is_free(dve, ("fl",))
            link(stt(az, zf, -1.0, zf, ALU.mult, ALU.max))
            sync()
            link(ts(az, az, -1.0, None, ALU.mult))
            sync()
            dve.drain().then_inc(dve_for_act, 1)
            upto(("k1", 0))
            dve.wait_ge(*act_a.next())
            stt(lf[:, 3, :], zf, 0.0, lf[:, 2, :], ALU.min, ALU.subtract).then_inc(dve_for_pe, 1)
            upto(("q1", 0))
            ready(dve, ("cum",))
            link(copy(cumT[0:FOX, 0, :], B(("cum",))[0:FOX, 0:T]))
            free(ts(cumT[0:FOX, 1, :], B(("cum",))[0:FOX, 0:T], -1.0, None, ALU.mult), ("cum",), "dve")
            dve.drain().then_inc(dve_for_pe, 1)
            attention(4, [("fox", h) for h in range(FOX)] + [("mem", 1, h) for h in range(4)],
                      list(range(NMB)) + [NMB, NMB + 1], FOX_TILES)
            is_free(dve, ("O", 18))
            low_signal()
            for c in range(4):
                upto(("o1", c))
            norm(4, x)
            ffn(1)
            dve.wait_ge(*gf_a.next(16))

            def block_input(i):
                stt(x[:, i, :], x[:, i, :], rstd[:, 9, i:i + 1], gfree[:, :], ALU.mult, ALU.mult).then_inc(x_new, 1)

            normed(9, x, block_input)
            norm(5, x)
            for h in range(RH):
                for name, dst in (("rq", qr), ("rk", kr)):
                    upto((name, h))
                    ready(dve, (name, h))
                    o = B((name, h))
                    sync()
                    link(tt(rm[:, 0, :], o[:, :], const("cossin"), ALU.mult))
                    ins = tt(rm[:, 1, :], o[:, :], const("sincos"), ALU.mult)
                    free(ins, (name, h), "dve")
                    is_free(dve, (name, h))
                    sync()
                    link(tt(dst[:, h, 0:T], rm[:, 0, 0:T], rm[:, 0, T:2 * T], ALU.subtract))
                    link(tt(dst[:, h, T:2 * T], rm[:, 1, 0:T], rm[:, 1, T:2 * T], ALU.add))
            dve.drain().then_inc(dve_for_pe, 1)

            def ret_low(h):
                for j in range(2):
                    dve.wait_ge(*hi_a.next(2))
                    for kk in range(2):
                        f = 4 * h + 2 * j + kk
                        ins = stt(ML[:, f, :], B(("ry", h, j))[:, kk * T:(kk + 1) * T], hgn[:, f:f + 1],
                                  MH[:, f, :].bitcast(F32), ALU.mult, ALU.subtract)
                    free(ins, ("ry", h, j), "dve")

            for h in range(RH):
                upto(("rv", h, 1))
                upto(("rg", h, 1))
                for i in range(TT):
                    dve.wait_ge(*act_a.next())
                    ins = stt(rgs[:, i, :], rth[:, i, :], 1.0, B(("rg", h, i, "out"))[:, :], ALU.add, ALU.mult)
                    free(ins, ("rg", h, i, "out"), "dve")
                ready(dve, ("rs", h))
                free(tt(sdt[:, h % 2, :], B(("rs", h))[:, 0:384], const("decay")[:, h * 384:(h + 1) * 384], ALU.mult), ("rs", h), "dve")
                a = 16 + 4 * (h % 2)
                for i in range(TT):
                    ready(dve, ("ro", h, i))
                    link(nc.vector.bn_stats(stat[:, 32 + 6 * i:38 + 6 * i], B(("ro", h, i))[:, :]))
                sync()
                for i in range(TT):
                    link(nc.vector.bn_aggr(stat[:, 24 + 2 * i:26 + 2 * i], stat[:, 32 + 6 * i:38 + 6 * i]))
                sync()
                for i in range(TT):
                    link(ts(stat[:, a + i:a + i + 1], stat[:, 25 + 2 * i:26 + 2 * i], RMS_EPS, None, ALU.add))
                sync()
                dve.drain().then_inc(gn_stat, 1)
                if h:
                    ret_low(h - 1)
                dve.wait_ge(*gn_a.next())
                is_free(dve, ("rg", h, 1, "out"))
                for i in range(TT):
                    free(ts(ry[:, i, :], B(("ro", h, i))[:, :], stat[:, 24 + 2 * i:25 + 2 * i], stat[:, a + 2 + i:a + 3 + i],
                            ALU.subtract, ALU.mult), ("ro", h, i), "dve")
                is_free(dve, ("ro", h, 1))
                for i in range(TT):
                    link(tt(ry[:, i, :], ry[:, i, :], rgs[:, i, :], ALU.mult))
                dve.drain().then_inc(dve_for_pe, 1)
            ret_low(RH - 1)
            for c in range(8):
                upto(("ro", c))
            ple(0)
            norm(7, x)
            for n in ("kc", "vc"):
                for j in range(2):
                    upto((n, j))

            def build(v, half):
                src = kvc[:, 4 * v:4 * v + 4, :].rearrange("p g (n l) -> p g l n", l=CMP_S)
                pos = col(("pe_k", "pe_v")[v])
                n = CMP_S - half
                dst = blocks[:, half * CMP_S:(half + 1) * CMP_S, v * 64:(v + 1) * 64].rearrange("p l (g n) -> p g l n", g=4)
                for g in range(4):
                    link(tt(dst[:, g, :, 0:n], src[:, g, :, half:CMP_S],
                            pos[:, half * CMP_S:(half + 1) * CMP_S].unsqueeze(2).to_broadcast([P, CMP_S, n]), ALU.add))

            def low_blocks(half):
                dve.wait_ge(*hi_a.next())
                a = slice(8 * half, 8 * half + 8)
                tt(ML[:, a, :], blocks.rearrange("p l c -> p (l c)").rearrange("p (a b) -> p a b", a=16)[:, a, :],
                   MH[:, a, :].bitcast(F32), ALU.subtract).then_inc(lo_done, 1)

            is_free(dve, ("vc", 1))
            link(nc.vector.memset(blocks[:, CMP_S:CMP_L, CMP_S - 1:P:CMP_S], 0.0))
            upto(("ks", 0))
            build(0, 1)
            upto(("ks", 1))
            build(1, 1)
            sync()
            dve.drain().then_inc(dve_for_act, 1)
            upto(("kw", 0))
            build(0, 0)
            upto(("kw", 1))
            low_blocks(1)
            upto(("vs", 0))
            build(1, 0)
            sync()
            dve.drain().then_inc(dve_for_act, 1)
            for key in (("vs", 1), ("vw", 0), ("vw", 1)):
                upto(key)
            low_blocks(0)
            dve.wait_ge(*act_a.next())
            link(ts(g3.rearrange("p i c -> p (i c)"), g3.rearrange("p i c -> p (i c)"), 0.5, 0.5, ALU.mult, ALU.add))
            sync()
            for i in range(TT):
                gv = g3[:, i, :].rearrange("p (h b) -> p h b", b=3)[:, :, 0]
                link(ts(gv, gv, const("rowvalid")[:, i:i + 1], None, ALU.mult))
            sync()
            for n in ("c1k", "c1v"):
                for j in CMP_ORDER:
                    upto((n, j))
            for j in range(4):
                upto(("c1k", j))
            for j in range(4):
                upto(("c1v", j))
            dve.wait_ge(*act_a.next())
            link(ts(hs, hs, 0.044715, 1.0, ALU.mult, ALU.add))
            sync()
            tt(hs, hs, hx, ALU.mult).then_inc(dve_for_act, 1)
            dve.wait_ge(*act_a.next())
            stt(hs, hth, 1.0, hx, ALU.add, ALU.mult).then_inc(dve_for_pe, 1)

            def gate(t):
                dve.wait_ge(*act_a.next())
                free(stt(gs[:, t % 2, :], nth, 1.0, B(("ng", t))[:, :], ALU.add, ALU.mult), ("ng", t), "dve")
                is_free(dve, ("ng", t))

            upto(("ng", 0))
            gate(0)
            for s in range(NSA_H + 2):
                e = s % 2
                if s >= 2:
                    h = s - 2
                    ready(dve, ("On", h))
                    free(stt(om[:, e, :], B(("On", h))[:, 0:T], 0.5, gs[:, (h // 2) % 2, e * T:e * T + T], ALU.mult, ALU.mult),
                         ("On", h), "dve")
                    is_free(dve, ("On", h))
                    dve.drain().then_inc(dve_for_act, 1)
                if s < NSA_H:
                    oS, oW = B(("Ss", s)), B(("Sw", s))
                    mx = stat[:, 64 + 6 * e:70 + 6 * e]
                    ready(dve, ("Sw", s))
                    link(nc.vector.tensor_reduce(mx[:, 0:2], oS[:, 384:416].rearrange("p (i c) -> p i c", i=2), AX_X, ALU.max))
                    for br, o in ((1, oS), (2, oW)):
                        link(nc.vector.tensor_reduce(mx[:, 2 * br:2 * br + 1], o[:, 0:P], AX_X, ALU.max))
                        link(nc.vector.tensor_reduce(mx[:, 2 * br + 1:2 * br + 2], o[:, P:384], AX_X, ALU.max))
                    sync()
                    ts(stat[:, 8 * e:8 * e + 6], mx, -P ** -0.5, None, ALU.mult).then_inc(max_done, 1)
                if s and s % 2 == 0 and s // 2 < 8:
                    gate(s // 2)
                if 0 <= s - 1 < NSA_H:
                    o = B(("Ts", s - 1))
                    ready(dve, ("Ts", s - 1))
                    link(copy(ptS, o[:, 0:384]))
                    free(copy(ptC[0:CMP_S, 0:P], o[0:CMP_S, 384:512]), ("Ts", s - 1), "dve")
                if s >= 2:
                    dve.wait_ge(*hi_a.next())
                    link(tt(ML[:, s - 2, :], om[:, e, :], MH[:, s - 2, :].bitcast(F32), ALU.subtract))
                if s < NSA_H:
                    is_free(dve, ("Sw", s))
                    rc, fac = stat[:, 32 + 12 * e:38 + 12 * e], stat[:, 38 + 12 * e:44 + 12 * e]
                    link(nc.vector.reciprocal(rc, stat[:, 16 + 8 * e:22 + 8 * e]))
                    sync()
                    gh = g3.rearrange("p i (h b) -> p h b i", b=3)[:, s, :, :]
                    link(tt(fac.rearrange("p (b i) -> p b i", b=3), rc.rearrange("p (b i) -> p b i", b=3), gh, ALU.mult))
                    sync()
                    for br, p in enumerate((pC, pS, pW)):
                        for i in range(TT):
                            if br == 0:
                                a, w = i * CMP_S, CMP_S
                            else:
                                a, w = (0, P) if i == 0 else (P, T)
                            ins = ts(p[:, e, a:a + w], p[:, e, a:a + w], fac[:, 2 * br + i:2 * br + i + 1], None, ALU.mult)
                    ins.then_inc(prob_done, 1)
                if s and (s + 1) // 2 < 8:
                    upto((("ng", "nq")[s % 2], (s + 1) // 2))
            sync()
            low_signal()
            for c in range(8):
                upto(("no", c))
            ple(1)
            dve.wait_ge(*gf_a.next(16))

            def output(i):
                stt(xn[:, i, :], x[:, i, :], rstd[:, 10, i:i + 1], gfree[:, :], ALU.mult, ALU.mult).then_inc(out_done, 1)

            normed(10, x, output)


def tile_of(w, kind, c0, k0=0):
    kb, cols = {"T": (8, 256), "N": (4, 512), "D": (2, 1024)}[kind]
    return w[k0:k0 + kb * P, c0:c0 + cols].reshape(kb, P, cols).transpose(1, 0, 2).reshape(P, kb * cols)


def weight_stream(a):
    def one(key):
        n = key[0]
        if n == "mk":
            return tile_of(a["w_mem_kv"][key[1]], "T", 0)
        if n == "mv":
            return tile_of(a["w_mem_kv"][key[1]], "T", 256)
        if n == "ca":
            return tile_of(a["w_in_a"][0], "T", 256 * key[1])
        if n == "cg":
            return tile_of(a["w_in_a"][0], "T", MIX + 256 * key[1])
        if n == "qm":
            return tile_of(a["w_in_a"][0], "T", 2 * MIX) if key[1] == 0 else tile_of(a["w_in_b"][0], "T", MIX)
        if n in ("o0", "o1"):
            return tile_of(a["w_out"][int(n[1])], "D", 0, 256 * key[1])
        if n == "fg":
            return tile_of(a["w_up"][key[1]], "T", 256 * key[2])
        if n == "fv":
            return tile_of(a["w_up"][key[1]], "T", DFF + 256 * key[2])
        if n == "fd":
            return tile_of(a["w_down"][key[1]], "D", 0, 256 * key[2])
        if n == "k1":
            return tile_of(a["w_kvf"], "T", 256 * key[1])
        if n == "v1":
            return tile_of(a["w_kvf"], "T", MIX + 256 * key[1])
        if n == "q1":
            return tile_of(a["w_in_b"][0], "T", 256 * key[1])
        if n == "rq":
            return tile_of(a["ret_w_in_2"][0], "T", 256 * key[1])
        if n == "rk":
            return tile_of(a["ret_w_in_2"][0], "T", 1024 + 256 * key[1])
        if n == "rv":
            return tile_of(a["ret_w_in_2"][0], "N", 2048 + 512 * key[1], 512 * key[2])
        if n == "rg":
            return tile_of(a["ret_w_in_2"][0], "N", 4096 + 512 * key[1], 512 * key[2])
        if n == "ro":
            return tile_of(a["ret_w_out_2"][0], "D", 0, 256 * key[1])
        if n == "pe":
            return tile_of(a["ple_w_emb_2"][key[1]], "D", 0)
        if n in ("pg0", "pg1"):
            return tile_of(a["ple_w_gate_2"][int(n[2])], "D", 0, 256 * key[1])
        if n in ("kc", "vc", "ks", "kw"):
            c = {"kc": 0, "vc": 512, "ks": 1024, "kw": 2048}[n]
            return tile_of(a["kv_w_2"], "T", c + 256 * key[1])
        if n in ("vs", "vw"):
            return tile_of(a["kv_w_2"], "N", {"vs": 1536, "vw": 2560}[n], 512 * key[1])
        if n in ("c1k", "c1v"):
            w = a["cmp_w1_k_2"] if n == "c1k" else a["cmp_w1_v_2"]
            return tile_of(w, "T", 0, 1024 * key[1])
        if n == "nq":
            return tile_of(a["nsa_w_in_2"][0], "T", 256 * key[1])
        if n == "ng":
            return tile_of(a["nsa_w_in_2"][0], "T", 2048 + 256 * key[1])
        return tile_of(a["nsa_w_out_2"][0], "D", 0, 256 * key[1])

    return np.stack([one(key) for key in TILES])


def param_array(a):
    def cols(v):
        return v.reshape(-1, P).T

    def wide(w):
        return w.reshape(-1, P, w.shape[1]).transpose(1, 0, 2).reshape(P, -1)

    v = {"g_mem": cols(a["g_mem"]), "g_kv": cols(a["g_kv"]), "ret_norm": cols(a["ret_norm_2"][0]),
         "kv_norm": cols(a["kv_norm_2"]), "nsa_norm": cols(a["nsa_norm_2"][0]), "b_glu": cols(a["b_glu"][0]),
         "b_dw_a": cols(a["b_dw_a"][0]), "ln_g": cols(a["ln_g"][0]), "ln_b": cols(a["ln_b"][0]),
         "w_dw_a": cols(a["w_dw_a"][0]), "ret_gn": cols(a["ret_gn_2"][0]), "pe_k": a["cmp_pe_k_2"].T,
         "pe_v": a["cmp_pe_v_2"].T, "w2_k": wide(a["cmp_w2_k_2"]), "w2_v": wide(a["cmp_w2_v_2"]),
         "w_f": wide(a["w_kvf"][:, 2 * MIX:]), "w_bg": wide(a["nsa_w_in_2"][0][:, 4096:])}
    for l in range(2):
        v[f"g_mix{l}"] = cols(a["g_mix"][l])
        v[f"g_ffn{l}"] = cols(a["g_ffn"][l])
        v[f"ple_norm{l}"] = cols(a["ple_norm_2"][l])
        v[f"w_dw_f{l}"] = cols(a["w_dw_f"][l])
        v[f"b_dw_f{l}"] = cols(a["b_dw_f"][l])
    return np.ascontiguousarray(np.concatenate([v[n] for n, _ in PARAM_PARTS], axis=1))


def const_array():
    f8 = np.float64
    half = 128
    inv = (np.float32(10000.0) ** (-np.arange(half, dtype=np.float32) / np.float32(half))).astype(np.float32)
    ang = (np.arange(T, dtype=np.float32)[None, :] * inv[:, None]).astype(f8)
    cos, sin = np.cos(ang), np.sin(ang)
    lg = np.log1p(-(2.0 ** (-5.0 - np.arange(RH, dtype=f8))))
    m, n = np.arange(P)[:, None], np.arange(P)[None, :]
    scale = 256.0 ** -0.5
    decay = []
    for h in range(RH):
        same = np.where(n >= m, np.exp(np.maximum(n - m, 0) * lg[h]), 0.0) * scale
        cross = np.exp((n + 1.0) * lg[h]) * np.exp((P - 1.0 - m) * lg[h]) * scale
        decay.append(np.concatenate([same, cross, same], axis=1))
    t = np.arange(T)
    tri = [8.0 * (np.arange(i * P, (i + 1) * P)[:, None] <= t[None, :]) for i in range(TT)]
    causal = np.where(n <= m, 0.0, NEG)
    cmpm = [np.where(((np.arange(CMP_S)[None, :] * CMP_S + CMP_L - 1 <= np.arange(i * P, (i + 1) * P)[:, None])
                      & (np.arange(CMP_S)[None, :] < CMP_S - 1))
                     | (np.arange(i * P, (i + 1) * P)[:, None] < CMP_L - 1), 0.0, NEG) for i in range(TT)]
    rowv = [(np.arange(i * P, (i + 1) * P)[:, None] >= CMP_L - 1) * 1.0 for i in range(TT)]
    v = {"cossin": np.concatenate([cos, sin], 1), "sincos": np.concatenate([sin, cos], 1),
         "decay": np.concatenate(decay, 1), "tri8": np.concatenate(tri, 1), "causal": causal,
         "cmpmask": np.concatenate(cmpm, 1), "rowvalid": np.concatenate(rowv, 1), "ones": np.full((P, P), 1.0 / MIX)}
    return np.ascontiguousarray(np.concatenate([v[n] for n, _ in CONST_PARTS], axis=1).astype(np.float32))


def kernel(**inputs):
    import concourse.bacc as bacc
    from concourse.bass_utils import run_bass_kernel_spmd

    a = {k: np.ascontiguousarray(v) for k, v in inputs.items()}
    arrays = {"wstream": weight_stream(a), "params": param_array(a), "consts": const_array(), "ident_in": np.eye(P, dtype=np.float32), "x_in": a["x"],
              "mem_in": a["mem"], "p_in": a["p_2"], "b_f": a["b_f"], "g_final": a["g_final"],
              "final_norm": a["final_norm_2"]}
    nc = bacc.Bacc("TRN2", target_bir_lowering=False, num_devices=1, dynamic_dma_scratch_size=1024)
    args = {n: nc.dram_tensor(n, v.shape, F32, kind="ExternalInput").ap() for n, v in arrays.items()}
    out = nc.dram_tensor("out_dram", (1, T, D), F32, kind="ExternalOutput").ap()
    program(nc, args["wstream"], args["params"], args["consts"], args["ident_in"], args["x_in"], args["mem_in"], args["p_in"], args["b_f"],
            args["g_final"], args["final_norm"], out)
    r = run_bass_kernel_spmd(nc, [arrays], core_ids=[0])
    return r.results[0]["out_dram"]
```
